# Optimizing a Trainium2 kernel written in Bass

```python
import math, functools
import jax, jax.numpy as jnp
from jax import lax
import numpy as np

D_MODEL = 2048
BATCH = 1
SEQ = 256
DEPTH = 1
DEC_BATCH = 8
DEC_SEQ = 8
PAST_LEN = 2048
PAGE_SIZE = 128

MIX_WIDTH = D_MODEL
LRU_WIDTH = MIX_WIDTH // 2
LRU_HEADS = 8
LRU_BLOCK = LRU_WIDTH // LRU_HEADS
CONV_W = 4
LRU_C = 8.0
ATTN_WIDTH = MIX_WIDTH - LRU_WIDTH
HEAD_DIM = 128
N_HEADS = ATTN_WIDTH // HEAD_DIM
N_KV_HEADS = 2
GROUP = N_HEADS // N_KV_HEADS
WINDOW = 128
ROPE_THETA = 10000.0
D_FF = 5504
N_MOD = 9
EPS = 1e-6
NEG = -1e30
IN_SPLITS = (LRU_WIDTH, 2 * LRU_WIDTH, 2 * LRU_WIDTH + N_HEADS * HEAD_DIM,
             2 * LRU_WIDTH + (N_HEADS + N_KV_HEADS) * HEAD_DIM)
IN_COLS = 2 * LRU_WIDTH + (N_HEADS + 2 * N_KV_HEADS) * HEAD_DIM

kernel_name = 'hymba_rglru_swa_macaron_step'

def _rmsnorm(x, g):
    xf = x.astype(jnp.float32)
    y = xf * lax.rsqrt(jnp.mean(xf * xf, axis=-1, keepdims=True) + EPS) * g.astype(jnp.float32)
    return y.astype(x.dtype)

def _swiglu(h, wg, wu, wd):
    return (jax.nn.silu(h @ wg) * (h @ wu)) @ wd

def _rope(x, pos):
    half = HEAD_DIM // 2
    inv = ROPE_THETA ** (-jnp.arange(half, dtype=jnp.float32) / half)
    ang = pos.astype(jnp.float32)[:, None] * inv[None, :]
    shape = (pos.shape[0],) + (1,) * (x.ndim - 3) + (half,)
    cos = jnp.cos(ang).reshape(shape)
    sin = jnp.sin(ang).reshape(shape)
    xf = x.astype(jnp.float32)
    x1, x2 = xf[..., :half], xf[..., half:]
    return jnp.concatenate([x1 * cos - x2 * sin, x2 * cos + x1 * sin], axis=-1).astype(x.dtype)

def _causal_conv(xb, buf, w, b):
    S = xb.shape[1]
    full = jnp.concatenate([buf.astype(xb.dtype), xb], axis=1)
    y = b
    for j in range(CONV_W):
        y = y + full[:, j:j + S] * w[j]
    return y, full[:, -(CONV_W - 1):]

def _combine(left, right):
    a1, b1 = left
    a2, b2 = right
    return a1 * a2, a2 * b1 + b2

def _rg_lru(xc, h0, w_a, b_a, w_x, b_x, lam):
    B, S, C = xc.shape
    xh = xc.reshape(B, S, LRU_HEADS, LRU_BLOCK)
    r = jax.nn.sigmoid(jnp.einsum('bshi,hij->bshj', xh, w_a) + b_a).reshape(B, S, C)
    gi = jax.nn.sigmoid(jnp.einsum('bshi,hij->bshj', xh, w_x) + b_x).reshape(B, S, C)
    log_a = -LRU_C * r.astype(jnp.float32) * jax.nn.softplus(-lam.astype(jnp.float32))
    a = jnp.exp(log_a)
    u = jnp.sqrt(-jnp.expm1(2.0 * log_a)) * (gi * xc).astype(jnp.float32)
    a_cum, h_cum = lax.associative_scan(_combine, (a, u), axis=1)
    h = a_cum * h0.astype(jnp.float32)[:, None, :] + h_cum
    return h.astype(xc.dtype), h[:, -1]

def _sink_attention(q, k, v, mask, sinks):
    s = jnp.einsum('...qkgd,...skd->...kgqs', q, k).astype(jnp.float32) * (HEAD_DIM ** -0.5)
    s = jnp.where(mask, s, NEG)
    sink = sinks.astype(jnp.float32).reshape(N_KV_HEADS, GROUP, 1, 1)
    m = jnp.maximum(jnp.max(s, axis=-1, keepdims=True), sink)
    p = jnp.exp(s - m)
    probs = p / (jnp.sum(p, axis=-1, keepdims=True) + jnp.exp(sink - m))
    return jnp.einsum('...kgqs,...skd->...qkgd', probs.astype(v.dtype), v)

def _attend_prompt(q, k, v, sinks):
    B, S = q.shape[0], q.shape[1]
    nb = S // WINDOW
    qb = q.reshape(B, nb, WINDOW, N_KV_HEADS, GROUP, HEAD_DIM)
    kb = k.reshape(B, nb, WINDOW, N_KV_HEADS, HEAD_DIM)
    vb = v.reshape(B, nb, WINDOW, N_KV_HEADS, HEAD_DIM)

    def band(t):
        prev = jnp.concatenate([jnp.zeros_like(t[:, :1]), t[:, :-1]], axis=1)
        return jnp.concatenate([prev, t], axis=2)

    qpos = jnp.arange(S).reshape(nb, WINDOW, 1)
    kpos = ((jnp.arange(nb)[:, None] - 1) * WINDOW + jnp.arange(2 * WINDOW)[None, :])[:, None, :]
    mask = (kpos <= qpos) & (kpos >= qpos - WINDOW) & (kpos >= 0)
    out = _sink_attention(qb, band(kb), band(vb), mask[None, :, None, None], sinks)
    return out.reshape(B, S, ATTN_WIDTH), k[:, -WINDOW:], v[:, -WINDOW:]

def _attend_sample(q, k, v, sinks, cache_k, cache_v):
    B, S = q.shape[0], q.shape[1]
    k_all = jnp.concatenate([cache_k.astype(k.dtype), k], axis=1)
    v_all = jnp.concatenate([cache_v.astype(v.dtype), v], axis=1)
    qpos = PAST_LEN + jnp.arange(S)[:, None]
    kpos = PAST_LEN - WINDOW + jnp.arange(WINDOW + S)[None, :]
    mask = (kpos <= qpos) & (kpos >= qpos - WINDOW)
    out = _sink_attention(q, k_all, v_all, mask[None, None, None], sinks)
    return out.reshape(B, S, ATTN_WIDTH), k_all[:, -WINDOW:], v_all[:, -WINDOW:]

def _layer(x, c, conv_buf, h0, pos, attend, p):
    (ada_w, ada_b, g1, g2, g3, f1g, f1u, f1d, w_in, conv_w, conv_b, wa, ba, wx, bx,
     lam, sinks, w_out, f2g, f2u, f2d) = p
    B, S, _ = x.shape
    mod = (jax.nn.silu(c) @ ada_w + ada_b).reshape(B, N_MOD, 1, D_MODEL)
    sh1, sc1, gt1, sh2, sc2, gt2, sh3, sc3, gt3 = [mod[:, i] for i in range(N_MOD)]
    h = _rmsnorm(x, g1) * (1 + sc1) + sh1
    x = x + 0.5 * gt1 * _swiglu(h, f1g, f1u, f1d)
    h = _rmsnorm(x, g2) * (1 + sc2) + sh2
    xb, yb, q, k, v = jnp.split(h @ w_in, IN_SPLITS, axis=-1)
    xc, conv_new = _causal_conv(xb, conv_buf, conv_w, conv_b)
    hs, h_last = _rg_lru(xc, h0, wa, ba, wx, bx, lam)
    lru_out = hs * jax.nn.gelu(yb)
    q = _rope(q.reshape(B, S, N_KV_HEADS, GROUP, HEAD_DIM), pos)
    k = _rope(k.reshape(B, S, N_KV_HEADS, HEAD_DIM), pos)
    v = v.reshape(B, S, N_KV_HEADS, HEAD_DIM)
    attn_out, k_new, v_new = attend(q, k, v, sinks)
    x = x + gt2 * (jnp.concatenate([lru_out, attn_out], axis=-1) @ w_out)
    h = _rmsnorm(x, g3) * (1 + sc3) + sh3
    x = x + 0.5 * gt3 * _swiglu(h, f2g, f2u, f2d)
    return x, conv_new, h_last, k_new, v_new

def setup_inputs(seed: int = 0) -> dict:
    key = jax.random.key(seed)
    ks = iter(jax.random.split(key, 40))
    f32 = jnp.float32
    L = DEPTH

    def nrm(shape, scale):
        return jax.random.normal(next(ks), shape, f32) * scale

    u = jax.random.uniform(next(ks), (L, LRU_WIDTH), f32, 0.9, 0.999)
    return {
        'x_prompt': nrm((BATCH, SEQ, D_MODEL), 1.0),
        'x_sample': nrm((DEC_BATCH, DEC_SEQ, D_MODEL), 1.0),
        'c_prompt': nrm((BATCH, D_MODEL), 1.0),
        'c_sample': nrm((DEC_BATCH, D_MODEL), 1.0),
        'state_conv': nrm((L, DEC_BATCH, CONV_W - 1, LRU_WIDTH), 1.0),
        'state_lru': nrm((L, DEC_BATCH, LRU_WIDTH), 0.5),
        'cache_k_win': nrm((L, DEC_BATCH, WINDOW, N_KV_HEADS, HEAD_DIM), 1.0),
        'cache_v_win': nrm((L, DEC_BATCH, WINDOW, N_KV_HEADS, HEAD_DIM), 1.0),
        'ada_w': nrm((L, D_MODEL, N_MOD * D_MODEL), 0.5 * D_MODEL ** -0.5),
        'ada_b': nrm((L, N_MOD * D_MODEL), 0.02),
        'norm_ffn1': 1.0 + nrm((L, D_MODEL), 0.05),
        'norm_mix': 1.0 + nrm((L, D_MODEL), 0.05),
        'norm_ffn2': 1.0 + nrm((L, D_MODEL), 0.05),
        'ffn1_w_gate': nrm((L, D_MODEL, D_FF), D_MODEL ** -0.5),
        'ffn1_w_up': nrm((L, D_MODEL, D_FF), D_MODEL ** -0.5),
        'ffn1_w_down': nrm((L, D_FF, D_MODEL), D_FF ** -0.5),
        'w_in': nrm((L, D_MODEL, IN_COLS), D_MODEL ** -0.5),
        'conv_w': nrm((L, CONV_W, LRU_WIDTH), CONV_W ** -0.5),
        'conv_b': nrm((L, LRU_WIDTH), 0.02),
        'lru_w_a': nrm((L, LRU_HEADS, LRU_BLOCK, LRU_BLOCK), LRU_BLOCK ** -0.5),
        'lru_b_a': nrm((L, LRU_HEADS, LRU_BLOCK), 0.02),
        'lru_w_x': nrm((L, LRU_HEADS, LRU_BLOCK, LRU_BLOCK), LRU_BLOCK ** -0.5),
        'lru_b_x': nrm((L, LRU_HEADS, LRU_BLOCK), 0.02),
        'lru_lambda': jnp.log(u) - jnp.log1p(-u),
        'attn_sinks': nrm((L, N_HEADS), 1.0),
        'w_out': nrm((L, MIX_WIDTH, D_MODEL), MIX_WIDTH ** -0.5),
        'ffn2_w_gate': nrm((L, D_MODEL, D_FF), D_MODEL ** -0.5),
        'ffn2_w_up': nrm((L, D_MODEL, D_FF), D_MODEL ** -0.5),
        'ffn2_w_down': nrm((L, D_FF, D_MODEL), D_FF ** -0.5),
        'norm_final': 1.0 + nrm((D_MODEL,), 0.05),
    }

def reference(x_prompt, x_sample, c_prompt, c_sample, state_conv, state_lru, cache_k_win, cache_v_win,
              ada_w, ada_b, norm_ffn1, norm_mix, norm_ffn2, ffn1_w_gate, ffn1_w_up, ffn1_w_down,
              w_in, conv_w, conv_b, lru_w_a, lru_b_a, lru_w_x, lru_b_x, lru_lambda, attn_sinks,
              w_out, ffn2_w_gate, ffn2_w_up, ffn2_w_down, norm_final):
    Bp, Sp = x_prompt.shape[0], x_prompt.shape[1]
    pos_p = jnp.arange(Sp)
    pos_s = PAST_LEN + jnp.arange(x_sample.shape[1])
    xp, xs = x_prompt, x_sample
    conv_p, lru_p, k_p, v_p = [], [], [], []
    conv_s, lru_s, k_s, v_s = [], [], [], []
    for l in range(DEPTH):
        p = (ada_w[l], ada_b[l], norm_ffn1[l], norm_mix[l], norm_ffn2[l], ffn1_w_gate[l], ffn1_w_up[l],
             ffn1_w_down[l], w_in[l], conv_w[l], conv_b[l], lru_w_a[l], lru_b_a[l], lru_w_x[l], lru_b_x[l],
             lru_lambda[l], attn_sinks[l], w_out[l], ffn2_w_gate[l], ffn2_w_up[l], ffn2_w_down[l])
        zero_conv = jnp.zeros((Bp, CONV_W - 1, LRU_WIDTH), x_prompt.dtype)
        zero_h = jnp.zeros((Bp, LRU_WIDTH), jnp.float32)
        xp, cp, hp, kp, vp = _layer(xp, c_prompt, zero_conv, zero_h, pos_p, _attend_prompt, p)
        attend_s = functools.partial(_attend_sample, cache_k=cache_k_win[l], cache_v=cache_v_win[l])
        xs, cs, hs, kss, vss = _layer(xs, c_sample, state_conv[l], state_lru[l], pos_s, attend_s, p)
        conv_p.append(cp); lru_p.append(hp); k_p.append(kp); v_p.append(vp)
        conv_s.append(cs); lru_s.append(hs); k_s.append(kss); v_s.append(vss)
    y_prompt = _rmsnorm(xp, norm_final)
    y_sample = _rmsnorm(xs, norm_final)
    return (y_prompt, y_sample,
            jnp.stack(conv_p), jnp.stack(lru_p), jnp.stack(k_p), jnp.stack(v_p),
            jnp.stack(conv_s), jnp.stack(lru_s), jnp.stack(k_s), jnp.stack(v_s))


_drawn_inputs = setup_inputs


def setup_inputs(seed=0):
    import zlib

    import numpy as np

    out = dict(_drawn_inputs(seed))
    spreads = {}
    factors = {'norm_ffn1': 7.835, 'norm_ffn2': 7.506, 'lru_b_a': 8.0, 'lru_b_x': 8.0, 'attn_sinks': 8.0}
    for name, (base, spread) in spreads.items():
        noise = np.random.default_rng([zlib.crc32(name.encode()), seed]).standard_normal(out[name].shape)
        drawn = base * np.exp(spread * noise) if base else spread * noise
        out[name] = __import__('jax').numpy.asarray(drawn.astype(out[name].dtype))
    for name, factor in factors.items():
        out[name] = (out[name] * factor).astype(out[name].dtype)
    return out
```

```python
from contextlib import ExitStack

import concourse.bass as bass
from concourse import mybir

ALU = mybir.AluOpType
ACT = mybir.ActivationFunctionType
AX = mybir.AxisListType
F32 = mybir.dt.float32
F32R = mybir.dt.float32r

P = 128
D = 2048
KB = D // P
SEQ = 256
NB = 8
DS = 8
SAMP = NB * DS
T = SEQ + SAMP
NC_ = NB + 1
D_FF = 5504
FB = D_FF // P
CB = 8
CHUNKS = FB // CB
TAIL = FB - CHUNKS * CB
LRU = 1024
LH = LRU // P
CONV = 4
NH = 8
NKV = 2
GRP = NH // NKV
WIN = 128
N_MOD = 9
EPS = 1e-6
SCALE = float(P) ** -0.5
GELU_C = 0.7978845608028654
PAST = 2048

RAW = 8
SPLIT = 4
UNIT = 1024
HB = UNIT // P
ACC = 4
TU = 2 * TAIL * P

U_F1 = 2 * 4 * 8
G_F1 = KB
CH_U = CB * 4 + KB
CH_G = CB * 2 + KB
MOD_U = 4 * 8
TAIL_U = TAIL * 4 + KB // 2
TAIL_G = TAIL * 2 + KB
U_MIX = U_F1 + CHUNKS * CH_U + 7 * MOD_U + TAIL_U
G_MIX = G_F1 + CHUNKS * CH_G + TAIL_G
MIX_BLOCKS = 4 + NKV * (GRP + 2 * GRP)
U_OUT = U_MIX + 2 * MIX_BLOCKS
G_OUT = G_MIX + MIX_BLOCKS + 2 * LH
U_F2 = U_OUT + 2 * KB
G_F2 = G_OUT + KB
U_END = U_F2 + CHUNKS * CH_U + TAIL_U
ACT_FREED = 4 * LH

X_OUT = (CHUNKS + 1) * KB
X_F2 = X_OUT + KB
H_BASE = (0, KB, 3 * KB)
Q = KB // 4
X_AT = 12
RMS_AT = X_AT + KB + 4
MOD_AT = [*range(RMS_AT + 4, RMS_AT + 4 + 2 * Q), *range(48, 48 + Q)]
SET_UP = 3


def mixer_plan():
    order = [(24 + kv, "k", kv, 0) for kv in range(NKV)] + [(26 + kv, "v", kv, 0) for kv in range(NKV)]
    for kv in range(NKV):
        order += [(16 + GRP * kv + h, "q", kv, h) for h in range(GRP)]
        for h in range(GRP):
            order += [(GRP * kv + h, "x", kv, h), (LH + GRP * kv + h, "y", kv, h)]
    groups, freed, by = [], [], {"V": G_MIX, "A": 0}
    for _, kind, _, _ in order:
        groups.append(G_MIX + len(freed))
        for _ in range(3 if kind == "y" else 1):
            who = "A" if kind in "xy" else "V"
            by[who] += 1
            freed.append((who, by[who]))
    return [o[0] for o in order], [o[1:] for o in order], groups, freed


MIX_ORDER, MIX_KIND, MIX_GROUP, MIX_FREED = mixer_plan()
PRM_DMAS = 14
TOK_DMAS = 2 + 2 * NB

C_NORM, C_CW, C_CB, C_BA, C_BX, C_LAM, C_ADAB = 0, 64, 96, 104, 112, 120, 128
C_SCONV = C_ADAB + N_MOD * KB
C_SLRU = C_SCONV + NB * 3 * LH
N_PRM = C_SLRU + NB * LH

INS = ['x_prompt', 'x_sample', 'c_prompt', 'c_sample', 'state_conv', 'state_lru', 'cache_k_win', 'cache_v_win',
       'ada_w', 'ada_b', 'norm_ffn1', 'norm_mix', 'norm_ffn2', 'ffn1_w_gate', 'ffn1_w_up', 'ffn1_w_down',
       'w_in', 'conv_w', 'conv_b', 'lru_w_a', 'lru_b_a', 'lru_w_x', 'lru_b_x', 'lru_lambda', 'attn_sinks',
       'w_out', 'ffn2_w_gate', 'ffn2_w_up', 'ffn2_w_down', 'norm_final', 'identity', 'tables']
OUTS = [('y_prompt', (1, SEQ, D)), ('y_sample', (NB, DS, D)),
        ('conv_prompt', (1, 1, 3, LRU)), ('lru_prompt', (1, 1, LRU)),
        ('k_prompt', (1, 1, WIN, NKV, P)), ('v_prompt', (1, 1, WIN, NKV, P)),
        ('conv_sample', (1, NB, 3, LRU)), ('lru_sample', (1, NB, LRU)),
        ('k_sample', (1, NB, WIN, NKV, P)), ('v_sample', (1, NB, WIN, NKV, P))]


def build(nc, io):
    ctx = ExitStack()
    with ctx:
        def sb(name, shape, dt=F32):
            return ctx.enter_context(nc.sbuf_tensor(name, shape, dt))

        def sem(name):
            return ctx.enter_context(nc.semaphore(name))

        raw = sb("raw", [P, RAW, UNIT])
        hi = sb("hi", [P, SPLIT, UNIT], F32R)
        lo = sb("lo", [P, SPLIT, UNIT], F32R)
        x = sb("x", [P, KB, T])
        h_hi = sb("h_hi", [P, KB, T], F32R)
        h_lo = sb("h_lo", [P, KB, T], F32R)
        mod = sb("mod", [P, N_MOD * KB, NC_])
        prm = sb("prm", [P, N_PRM])
        ident = sb("ident", [P, P])
        ones = sb("ones", [P, P])[:, :]
        c_split = sb("c_split", [P, KB, 2 * NC_], F32R)
        small = sb("small", [P, 96])
        with nc.sbuf_tensor("a_hi", [P, CB, T], F32R) as a_hi, nc.sbuf_tensor("a_lo", [P, CB, T], F32R) as a_lo:
            pass
        work = sb("work", [P, 18990])

        def carve(at, *shape):
            n = 1
            for s in shape:
                n *= s
            v = work[:, at:at + n]
            if len(shape) == 2:
                v = v.rearrange("p (a b) -> p a b", b=shape[1])
            if len(shape) == 3:
                v = v.rearrange("p (a b c) -> p a b c", b=shape[1], c=shape[2])
            return v, at + n

        at = 2 * CB * T
        silu_g, at = carve(at, 2, T)
        prod, at = carve(at, 2, T)
        xn, at = carve(at, 3, T)
        h_samp, at = carve(at, KB, SAMP)
        mod_row, at = carve(at, 512)
        rstd, at = carve(at, T)
        ln_ms, at = carve(at, T)
        sum_sq, at = carve(at, T)
        sq, ffn_end = carve(at, 2, T)
        x_tok, _ = carve(0, 3, D)
        c_tok, _ = carve(3 * D, D)
        prm_tok, at2 = carve(11072, 5, P)
        y_tok, _ = carve(0, 3, D)
        mix, at = carve(0, KB, T)
        k_t, at = carve(at, NKV, T)
        swapped, at = carve(at, T)
        ck_t, at = carve(at, NB, P)
        q_p, at = carve(at, GRP, SEQ)
        q_s, at = carve(at, NB, GRP, DS)
        tok, at = carve(at, 5, NKV, P)
        score, at = carve(at, 3 * P)
        probs_t, at = carve(at, 3 * P)
        rope_c, rope_s = score[:, 0:T], probs_t[:, 0:T]
        v_t, _ = carve(at, NKV, T)
        xb_p, at = carve(at, 3 + SEQ)
        xb_s, at = carve(at, NB, 3 + DS)
        xc2, at = carve(at, 2, T)
        yf, at = carve(at, T)
        gel, at = carve(at, T)
        th_r, at = carve(at, T)
        th_x, at = carve(at, T)
        root, at = carve(at, T)
        a_p, at = carve(at, SEQ)
        a_s, at = carve(at, NB, 1 + DS)
        u_p, at = carve(at, SEQ)
        u_s, at = carve(at, NB, 1 + DS)
        hs_p, at = carve(at, SEQ)
        hs_s, at = carve(at, NB, 1 + DS)
        st, at = carve(at, 288)
        early = at
        tables, at = carve(at, 2 * 3 * P + 4 + 2 * T)
        ck_tok, at = carve(at, NB, P)
        cv_tok, at = carve(at, NB, P)
        w_a, at = carve(at, GRP, P)
        w_x, at = carve(at, GRP, P)
        assert at <= 18990 and early >= ffn_end, (at, early)
        mask_p = tables[:, 0:3 * P]
        mask_s = [tables[:, 3 * P + (P + SAMP) * b:3 * P + (P + SAMP) * (b + 1)] for b in range(2)]
        group_of = tables[:, 6 * P:6 * P + 4]
        cos = tables[:, 6 * P + 4:6 * P + 4 + T]
        sin = tables[:, 6 * P + 4 + T:6 * P + 4 + 2 * T]
        sinks = small[:, 0:8]
        sink_s = small[:, 8:10]
        m2sp = small[:, 10:18]
        m4sp = small[:, 18:26]
        half_ba = small[:, 26:34]
        half_bx = small[:, 34:42]
        top = small[:, 42:44]
        neg_top = small[:, 44:46]
        den = small[:, 46:48]
        sink_e = small[:, 48:50]
        sp_e = small[:, 50:58]
        sp_q = small[:, 58:66]
        sp_s = small[:, 66:74]
        sink_pick = small[:, 74:78]
        eps = small[:, 78:79]
        warm = small[:, 79:80]
        final_norm = small[:, 80:96]

        psum = ctx.enter_context(nc.psum_tensor("ps", [P, 8, 512], F32))
        acc = [psum[:, b, 0:T] for b in range(ACC)]
        B_MOD, B_MODT, B_NORM = 4, 6, 7
        B_SCORE, B_PT, B_TOK, B_O = 4, 5, 6, 7

        landed = [sem(f"landed{i}") for i in range(RAW)]
        hi_done = sem("hi_done")
        lo_done = sem("lo_done")
        unit_done = sem("unit_done")
        dve_freed = sem("dve_freed")
        act_freed = sem("act_freed")
        c_in, prm_in, ident_in, x_in, tables_in = map(sem, ("c_in", "prm_in", "ident_in", "x_in", "tables_in"))
        ck_in, cv_in, gates_in, sinks_in = map(sem, ("ck_in", "cv_in", "gates_in", "sinks_in"))
        set_up = sem("set_up")
        c_silu, c_turned, prm_turned, c_ready, prm_ready = map(sem, ("c_silu", "c_turned", "prm_turned", "c_ready", "prm_ready"))
        x_turned = sem("x_turned")
        mod_row_ready = sem("mod_row_ready")
        mod_turned = sem("mod_turned")
        mod_half = sem("mod_half")
        mod_done = sem("mod_done")
        x_done = sem("x_done")
        squared = sem("squared")
        summed = sem("summed")
        ms_ready, rstd_ready = sem("ms_ready"), sem("rstd_ready")
        scale_ready = sem("scale_ready")
        xn_ready, h_hi_ready, h_ready = map(sem, ("xn_ready", "h_hi_ready", "h_ready"))
        samp_ready, samp_hi_ready, samp_lo_ready = map(sem, ("samp_ready", "samp_hi_ready", "samp_lo_ready"))
        silu_ready, a_hi_ready, a_ready = map(sem, ("silu_ready", "a_hi_ready", "a_ready"))
        swapped_ready, rope_done, tok_turned, tok_ready, tok_stored = map(
            sem, ("swapped_ready", "rope_done", "tok_turned", "tok_ready", "tok_stored"))
        ck_turned, ck_ready = sem("ck_turned"), sem("ck_ready")
        scored, masked, maxed, exp_done, probs_ready, pt_turned, pt_copied, o_ready, o_copied = map(
            sem, ("scored", "masked", "maxed", "exp_done", "probs_ready", "pt_turned", "pt_copied", "o_ready", "o_copied"))
        xc_ready, gates_ready, gate_acts, gel_z, gel_t, lru_done, state_saved = map(
            sem, ("xc_ready", "gates_ready", "gate_acts", "gel_z", "gel_t", "lru_done", "state_saved"))
        gelu_ready = sem("gelu_ready")
        xb_state = sem("xb_state")
        xn_y, y_turned, y_copied = sem("xn_y"), sem("y_turned"), sem("y_copied")
        st_turned, st_copied = sem("st_turned"), sem("st_copied")
        sp_ready, sp_exp = sem("sp_ready"), sem("sp_exp")
        act_chain, dve_chain, pool_chain = sem("act_chain"), sem("dve_chain"), sem("pool_chain")
        stored = sem("stored")
        cache_stored, state_stored = sem("cache_stored"), sem("state_stored")

        def plus(n, turns, per):
            return n if turns is None else turns * per + n

        def raw_slot(u):
            return raw[:, u % RAW, :]

        def hi_slot(u):
            return hi[:, u % SPLIT, :]

        def lo_slot(u):
            return lo[:, u % SPLIT, :]

        def bank(g):
            return acc[g % ACC]

        def sample(v):
            return v[:, SEQ:T].rearrange("p (b s) -> p b s", s=DS)

        def unit_floats(u):
            for end in (U_MIX, U_END):
                if end - KB // 2 <= u < end:
                    return TU
            return UNIT

        block = ctx.enter_context(nc.Block())

        @block.sync
        def _(sp):
            def load(u, turns, src, shape=(HB, P)):
                if u >= RAW or turns is not None:
                    sp.wait_ge(lo_done, plus(u - RAW + 1, turns, RAW))
                dst = raw_slot(u)[:, 0:shape[0] * shape[1]].rearrange("p (k n) -> p k n", n=shape[1])
                sp.dma_start(dst, src).then_inc(landed[u % RAW], 16)

            def blocks(w):
                return w.rearrange("(k p) n -> p k n", p=P)

            ada = blocks(io['ada_w'][0])

            def mod_unit(u, turns, group, part):
                load(u, turns, ada[:, 2 * part:2 * part + 2, bass.ds(group * 512, 512)], (2, 512))

            def columns(u, turns, w, half, col):
                load(u, turns, w[:, half * HB:(half + 1) * HB, bass.ds(col, P)])

            for part in range(16):
                mod_unit(part, None, part // 8 * Q, part % 8)
            with sp.Fori(0, 3) as i:
                for part in range(16):
                    mod_unit(16 + part, i * 2, i + (1 + part // 8 * Q), part % 8)

            def ffn(u0, gate, up, down, with_mod):
                gate, up, down = blocks(gate), blocks(up), blocks(down)

                def up_pair(u, turns, col, group):
                    for n in range(8):
                        w = (gate, up)[n // 2 % 2]
                        if group is not None:
                            mod_unit(u, turns, group, n)
                            u += 1
                        columns(u, turns, w, n % 2, col + P * (n // 4))
                        u += 1

                def down_eight(u, turns, row, col, group):
                    for n in range(8):
                        if group is not None:
                            for k in range(2):
                                part = 2 * n + k
                                mod_unit(u, turns, group + part // 8, part % 8)
                                u += 1
                        load(u, turns, down[:, bass.ds(row, CB), bass.ds(col + P * n, P)])
                        u += 1

                def chunk(u, chunk_turns, c, group, mod_up, mod_down):
                    per = 2 if mod_up else 1
                    with sp.Fori(0, 4) as i:
                        up_pair(u, chunk_turns + i * per, c * (CB * P) + i * (2 * P), group + i if mod_up else None)
                    u += CB * 4 * per
                    per = 3 if mod_down else 1
                    with sp.Fori(0, 2) as i:
                        down_eight(u, chunk_turns + i * per, c * CB, i * (CB * P),
                                   group + 4 + i * 2 if mod_down else None)
                    return u + KB + (2 * KB if mod_down else 0)

                if with_mod:
                    with sp.Fori(0, 3) as c:
                        chunk(u0, c * 14, c, c * 8 + 8, True, True)
                    u = chunk(u0 + 3 * 112, 0, 3, 32, True, False)
                    u = chunk(u, 0, 4, 0, False, False)
                else:
                    with sp.Fori(0, CHUNKS) as c:
                        chunk(u0, c * 6, c, 0, False, False)
                    u = u0 + CHUNKS * CH_U
                for s in range(TAIL):
                    for n in range(4):
                        columns(u, None, (gate, up)[n // 2], n % 2, (CHUNKS * CB + s) * P)
                        u += 1
                for n in range(KB // 2):
                    load(u, None, down[:, CHUNKS * CB:FB, n * 2 * P:(n + 1) * 2 * P], (TAIL, 2 * P))
                    u += 1

            ffn(U_F1, io['ffn1_w_gate'][0], io['ffn1_w_up'][0], io['ffn1_w_down'][0], True)

            w_in = blocks(io['w_in'][0])
            for n, col in enumerate(MIX_ORDER):
                for half in range(2):
                    columns(U_MIX + 2 * n + half, None, w_in, half, col * P)
                if n == 12:
                    sp.wait_ge(tok_ready, NKV)
                    sp.dma_start(io['v_prompt'][0, 0], tok[:, 1]).then_inc(tok_stored, 16)
                    sp.dma_start(io['k_prompt'][0, 0], tok[:, 3]).then_inc(tok_stored, 16)
                    for b in range(NB):
                        rows = slice(b * DS, (b + 1) * DS)
                        sp.dma_start(io['v_sample'][0, b, WIN - DS:], tok[rows, 2]).then_inc(tok_stored, 16)
                        sp.dma_start(io['k_sample'][0, b, WIN - DS:], tok[rows, 4]).then_inc(tok_stored, 16)

            w_out = blocks(io['w_out'][0])
            with sp.Fori(0, 4) as i:
                for m in range(4):
                    u = U_OUT + 2 * m
                    sp.wait_ge(lo_done, plus(u + 1 - RAW + 1, i, RAW))
                    for half in range(2):
                        sp.dma_start(raw_slot(u + half).rearrange("p (k n) -> p k n", n=P),
                                     w_out[:, (1 - half) * HB:(2 - half) * HB, bass.ds(i * (4 * P) + P * m, P)])\
                          .then_inc(landed[(u + half) % RAW], 16)

            ffn(U_F2, io['ffn2_w_gate'][0], io['ffn2_w_up'][0], io['ffn2_w_down'][0], False)

            ys = io['y_sample'].rearrange("b s n -> (b s) n")
            for q in range(4):
                sp.wait_ge(y_copied, 4 * (q + 1))
                cols = slice(4 * q * P, 4 * (q + 1) * P)
                for t in range(2):
                    sp.dma_start(io['y_prompt'][0, t * P:(t + 1) * P, cols], y_tok[:, t, cols]).then_inc(stored, 16)
                sp.dma_start(ys[:, cols], y_tok[0:SAMP, 2, cols]).then_inc(stored, 16)
            sp.wait_ge(stored, 12 * 16)
            sp.wait_ge(tok_stored, TOK_DMAS * 16)
            sp.wait_ge(cache_stored, 2 * 16)
            sp.wait_ge(state_stored, 5 * 16)

        @block.tensor
        def _(pe):
            mm = nc.tensor.matmul

            def turn(out, in_, n):
                return nc.tensor.transpose(out, in_, ident[0:n, 0:n])

            def arrive(u, turns):
                pe.wait_ge(lo_done, plus(u + 1, turns, RAW))

            def free_bank(g, gturns, freed_before=0):
                if g - ACC - freed_before >= 0 or gturns is not None:
                    pe.wait_ge(dve_freed, plus(g - ACC + 1 - freed_before, gturns, ACC))

            def products(out, u, j, cols, col, r_hi, r_lo, first, last):
                w_hi = hi_slot(u)[:, j * cols + col:j * cols + col + P]
                w_lo = lo_slot(u)[:, j * cols + col:j * cols + col + P]
                mm(out, w_hi, r_hi, start=first, stop=False)
                mm(out, w_hi, r_lo, start=False, stop=False)
                return mm(out, w_lo, r_hi, start=False, stop=last)

            def mod_unit(u, turns, part, group):
                arrive(u, turns)
                if part == 0 and group is not None:
                    pe.wait_ge(mod_row_ready, group)
                for j in range(2):
                    for w in range(2):
                        operand = (hi_slot(u), lo_slot(u))[w]
                        last = mm(psum[0:2 * NC_, B_MOD, :], c_split[:, 2 * part + j, :],
                                  operand[:, j * 512:(j + 1) * 512],
                                  start=(part == 0 and j == 0 and w == 0), stop=(part == 7 and j == 1 and w == 1))
                last.then_inc(unit_done, 1)

            def mod_turn(group):
                pe.wait_ge(mod_row_ready, group + 1)
                if not isinstance(group, int) or group > 0:
                    pe.wait_ge(mod_done, group)
                for j in range(4):
                    last = turn(psum[:, B_MODT, j * P:(j + 1) * P], mod_row[:, j * P:(j + 1) * P], P)
                last.then_inc(mod_turned, 1)

            pe.wait_ge(ident_in, 16)
            pe.wait_ge(c_silu, 1)
            for k in range(KB):
                last = turn(psum[:, 5, NC_ * k:NC_ * (k + 1)], c_tok[0:NC_, k * P:(k + 1) * P], NC_)
            last.then_inc(c_turned, 1)
            def turn_parameters():
                pe.wait_ge(prm_in, PRM_DMAS * 16)
                for k in range(4):
                    turn(psum[:, B_NORM, P * k:P * (k + 1)], prm_tok[:, k, :], P)
                turn(psum[:, B_MODT, 0:16], prm_tok[0:16, 4, :], 16).then_inc(prm_turned, 1)

            def turn_x(k):
                if k >= ACC:
                    pe.wait_ge(dve_freed, k - ACC + 1)
                for t in range(2):
                    turn(bank(k)[:, t * P:(t + 1) * P], x_tok[:, t, k * P:(k + 1) * P], P)
                turn(bank(k)[:, SEQ:T], x_tok[0:SAMP, 2, k * P:(k + 1) * P], SAMP).then_inc(x_turned, 1)

            def sum_of_squares(n):
                pe.wait_ge(summed, n * KB + KB)
                mm(psum[:, B_NORM, 0:T], ones, sum_sq, start=True, stop=True).then_inc(ms_ready, 1)

            pe.wait_ge(c_ready, 1)
            for g in range(8):
                for part in range(8):
                    mod_unit(8 * g + part, None, part, g if g else None)
                    k = 8 * g + part - X_AT
                    if k == 0:
                        pe.wait_ge(x_in, 3 * 16)
                    if 0 <= k < KB:
                        turn_x(k)
                    if 8 * g + part == RMS_AT:
                        sum_of_squares(0)
                if g == 0:
                    turn_parameters()
                    pe.wait_ge(prm_ready, 1)
                mod_turn(g)

            def project(u, turns, g, gturns, h0, freed_before=0, first=0):
                out = bank(g)
                for half in range(2):
                    arrive(u + half, turns)
                    if half == 0 and freed_before is not None:
                        free_bank(g, gturns, freed_before)
                    for j in range(HB):
                        n = half * HB + j
                        k = (first + n) % KB
                        pe.wait_ge(h_ready, h0 + n + 1)
                        last = products(out, u + half, j, P, 0, h_hi[:, k, :], h_lo[:, k, :], n == 0, n == KB - 1)
                    last.then_inc(unit_done, 1)

            def ffn(u0, g0, h0, a0, freed_before, with_mod):
                def up_pair(u, turns, g, gturns, group):
                    n = 0
                    for step in range(2):
                        for w in range(2):
                            out = bank(g)
                            for half in range(2):
                                if group is not None:
                                    mod_unit(u, turns, n, group)
                                    u += 1
                                arrive(u, turns)
                                if half == 0:
                                    free_bank(g, gturns, freed_before)
                                for j in range(HB):
                                    k = half * HB + j
                                    pe.wait_ge(h_ready, h0 + k + 1)
                                    last = products(out, u, j, P, 0, h_hi[:, k, :], h_lo[:, k, :], k == 0, k == KB - 1)
                                last.then_inc(unit_done, 1)
                                u += 1
                                n += 1
                            g += 1
                    if group is not None:
                        mod_turn(group)

                def down_eight(u, turns, g, gturns, a_before, group):
                    for n in range(8):
                        if group is not None:
                            for k in range(2):
                                part = 2 * n + k
                                mod_unit(u, turns, part % 8, group + part // 8)
                                u += 1
                        arrive(u, turns)
                        free_bank(g, gturns, freed_before)
                        for j in range(CB):
                            pe.wait_ge(a_ready, a_before + (j + 1))
                            last = products(bank(g), u, j, P, 0, a_hi[:, j, :], a_lo[:, j, :], j == 0, j == CB - 1)
                        last.then_inc(unit_done, 1)
                        u += 1
                        g += 1
                        if group is not None and n % 4 == 3:
                            mod_turn(group + n // 4)

                def chunk(u, turns, g, gturns, a_before, group, mod_up, mod_down):
                    per = 2 if mod_up else 1
                    with pe.Fori(0, 4) as i:
                        up_pair(u, turns + i * per, g, gturns + i, group + i if mod_up else None)
                    u, g = u + CB * 4 * per, g + 2 * CB
                    per = 3 if mod_down else 1
                    with pe.Fori(0, 2) as i:
                        down_eight(u, turns + i * per, g, gturns + i * 2, a_before,
                                   group + 4 + i * 2 if mod_down else None)
                    return u + KB + (2 * KB if mod_down else 0), g + KB

                if with_mod:
                    with pe.Fori(0, 3) as c:
                        chunk(u0, c * 14, g0, c * 8, c * CB + a0, c * 8 + 8, True, True)
                    u, g = chunk(u0 + 3 * 112, 0, g0 + 3 * CH_G, 0, a0 + 3 * CB, 32, True, False)
                    u, g = chunk(u, 0, g, 0, a0 + 4 * CB, 0, False, False)
                else:
                    with pe.Fori(0, CHUNKS) as c:
                        chunk(u0, c * 6, g0, c * 8, c * CB + a0, 0, False, False)
                    u, g = u0 + CHUNKS * CH_U, g0 + CHUNKS * CH_G
                for s in range(2 * TAIL):
                    project(u, None, g, None, h0, freed_before)
                    u, g = u + 2, g + 1
                for n in range(KB // 2):
                    arrive(u, None)
                    for m in range(2):
                        free_bank(g, None, freed_before)
                        for j in range(TAIL):
                            pe.wait_ge(a_ready, a0 + CHUNKS * CB + j + 1)
                            last = products(bank(g), u, j, 2 * P, m * P, a_hi[:, j, :], a_lo[:, j, :], j == 0,
                                            j == TAIL - 1)
                        g += 1
                    last.then_inc(unit_done, 1)
                    u += 1

            ffn(U_F1, G_F1, 0, 0, 0, True)
            sum_of_squares(1)

            def mix_project(n):
                g = MIX_GROUP[n]
                freed_sem, count = MIX_FREED[g - ACC - G_MIX] if g - ACC >= G_MIX else ("V", g - ACC + 1)
                pe.wait_ge(dve_freed if freed_sem == "V" else act_freed, count)
                project(U_MIX + 2 * n, None, g, None, KB, None)

            def token_major(kv):
                pe.wait_ge(rope_done, kv + 1)
                pe.wait_ge(dve_freed, MIX_FREED[2 + kv][1])
                if kv:
                    pe.wait_ge(tok_ready, kv)
                turn(psum[:, B_TOK, 0:P], v_t[:, kv, 0:P], P)
                turn(psum[:, B_TOK, P:2 * P], v_t[:, kv, P:2 * P], P)
                turn(psum[:, B_TOK, 2 * P:3 * P], k_t[:, kv, P:2 * P], P)
                turn(psum[0:SAMP, B_TOK, 3 * P:4 * P], v_t[:, kv, SEQ:T], P)
                turn(psum[0:SAMP, B_O, 0:P], k_t[:, kv, SEQ:T], P).then_inc(tok_turned, 1)

            def cached_keys(kv, half):
                pe.wait_ge(ck_in, 16 * (kv + 1))
                n = 2 * kv + half
                if n:
                    pe.wait_ge(ck_ready, n)
                if half == 0 and kv:
                    pe.wait_ge(pt_copied, 6 * kv)
                for b in range(4):
                    last = turn(psum[:, B_PT, b * P:(b + 1) * P], ck_tok[:, 4 * half + b, :], P)
                last.then_inc(ck_turned, 1)

            def scores(kv, t):
                job = 6 * kv + t
                if t == 0:
                    pe.wait_ge(rope_done, NKV + GRP * (kv + 1))
                    pe.wait_ge(ck_ready, 2 * (kv + 1))
                if job:
                    pe.wait_ge(masked, job)
                out = psum[:, B_SCORE, :]
                if t < GRP:
                    mm(out[:, 0:P], q_p[:, t, 0:P], k_t[:, kv, 0:P], start=True, stop=True)
                    last = mm(out[:, P:3 * P], q_p[:, t, P:SEQ], k_t[:, kv, 0:SEQ], start=True, stop=True)
                else:
                    b0 = 4 * (t - GRP)
                    for b in range(4):
                        mm(out[32 * b:32 * b + 32, 0:P], q_s[:, b0 + b, :, :].rearrange("p g s -> p (g s)"),
                           ck_t[:, b0 + b, :], start=True, stop=True)
                    last = mm(out[:, P:P + SAMP], q_s[:, b0:b0 + 4, :, :].rearrange("p b g s -> p (b g s)"),
                              k_t[:, kv, SEQ:T], start=True, stop=True)
                last.then_inc(scored, 1)

            def turn_probs(kv, t):
                job = 6 * kv + t
                pe.wait_ge(probs_ready, job + 1)
                if job:
                    pe.wait_ge(pt_copied, job)
                if t == 0:
                    pe.wait_ge(ck_ready, 2 * (kv + 1))
                out = psum[:, B_PT, :]
                if t < GRP:
                    for j in range(3):
                        last = turn(out[:, j * P:(j + 1) * P], score[:, j * P:(j + 1) * P], P)
                else:
                    turn(out[:, 0:P], score[:, 0:P], P)
                    last = turn(out[0:SAMP, P:2 * P], score[:, P:P + SAMP], P)
                last.then_inc(pt_turned, 1)

            def values(kv, t):
                job = 6 * kv + t
                pe.wait_ge(pt_copied, job + 1)
                if job:
                    pe.wait_ge(o_copied, job)
                if t == 0:
                    pe.wait_ge(tok_ready, NKV)
                out = psum[:, B_O, :]
                if t < GRP:
                    mm(out[:, 0:P], tok[:, 0, kv, :], probs_t[:, 0:P], start=True, stop=True)
                    mm(out[:, P:2 * P], tok[:, 0, kv, :], probs_t[:, P:2 * P], start=True, stop=False)
                    last = mm(out[:, P:2 * P], tok[:, 1, kv, :], probs_t[:, 2 * P:3 * P], start=False, stop=True)
                else:
                    if t == GRP:
                        pe.wait_ge(cv_in, 16 * (kv + 1))
                    mm(out[:, 0:P], tok[0:SAMP, 2, kv, :], probs_t[0:SAMP, P:2 * P], start=True, stop=False)
                    for b in range(4):
                        last = mm(out[:, 32 * b:32 * b + 32], cv_tok[:, 4 * (t - GRP) + b, :],
                                  probs_t[:, 32 * b:32 * b + 32], start=False, stop=(b == 3))
                last.then_inc(o_ready, 1)

            def attend(kv, t):
                if t >= 2:
                    values(kv, t - 2)
                if 1 <= t <= 6:
                    turn_probs(kv, t - 1)
                if t < 6:
                    scores(kv, t)

            def gates(kv, h, n):
                head = GRP * kv + h
                pe.wait_ge(xc_ready, head + 1)
                if h == 0:
                    pe.wait_ge(gates_in, 32 * (kv + 1))
                for k, w in enumerate((w_a, w_x)):
                    g = MIX_GROUP[n] + 1 + k
                    freed_sem, count = MIX_FREED[g - ACC - G_MIX]
                    pe.wait_ge(dve_freed if freed_sem == "V" else act_freed, count)
                    last = mm(bank(g), w[:, h, :], xc2[:, head % 2, :], start=True, stop=True)
                last.then_inc(gates_ready, 1)

            for n in range(4):
                mix_project(n)
            n = 4
            for kv in range(NKV):
                for q in range(GRP):
                    mix_project(n)
                    n += 1
                    if q < 2:
                        if kv == 0:
                            token_major(q)
                        cached_keys(kv, q)
                for h in range(GRP):
                    mix_project(n)
                    n += 1
                    attend(kv, 2 * h)
                    mix_project(n)
                    gates(kv, h, n)
                    n += 1
                    attend(kv, 2 * h + 1)

            pe.wait_ge(act_freed, ACT_FREED)
            with pe.Fori(0, 4) as i:
                for m in range(4):
                    project(U_OUT + 2 * m, i, G_OUT + m, i, 2 * KB, ACT_FREED, LH)

            pe.wait_ge(state_saved, LH)
            for t in range(2):
                turn(psum[:, B_SCORE, t * P:(t + 1) * P], st[:, t * P:(t + 1) * P], P)
            turn(psum[0:32, B_SCORE, 2 * P:3 * P], st[:, 2 * P:2 * P + 32], P).then_inc(st_turned, 1)

            sum_of_squares(2)
            ffn(U_F2, G_F2, 3 * KB, FB, ACT_FREED, False)
            sum_of_squares(3)

            for k in range(KB):
                pe.wait_ge(xn_y, k + 1)
                if k >= 2:
                    pe.wait_ge(y_copied, k - 1)
                out = psum[:, 4 + k % 2, :]
                for t in range(2):
                    turn(out[:, t * P:(t + 1) * P], xn[:, k % 3, t * P:(t + 1) * P], P)
                turn(out[0:SAMP, 2 * P:3 * P], xn[:, k % 3, SEQ:T], P).then_inc(y_turned, 1)

        @block.scalar
        def _(act):
            run = nc.scalar.activation
            chained = [0]

            def chain(instruction):
                chained[0] += 1
                instruction.then_inc(act_chain, 1)
                act.wait_ge(act_chain, chained[0])

            def split(u, turns=None):
                n = unit_floats(u)
                act.wait_ge(landed[u % RAW], plus(16 * (u // RAW + 1), turns, 16))
                run(hi_slot(u)[:, 0:n], raw_slot(u)[:, 0:n], ACT.Copy).then_inc(hi_done, 1)

            def finished(u, turns=None):
                act.wait_ge(unit_done, plus(u + 1, turns, RAW))

            def copy_mod():
                run(mod_row[0:2 * NC_, :], psum[0:2 * NC_, B_MOD, :], ACT.Copy).then_inc(mod_row_ready, 1)

            act.dma_start(c_tok[0:1, :], io['c_prompt']).then_inc(c_in, 16)
            act.dma_start(c_tok[1:NC_, :], io['c_sample']).then_inc(c_in, 16)
            act.dma_start(ident[:, :], io['identity']).then_inc(ident_in, 16)
            for t in range(2):
                act.dma_start(x_tok[:, t, :], io['x_prompt'][0, t * P:(t + 1) * P, :]).then_inc(x_in, 16)
            act.dma_start(x_tok[0:SAMP, 2, :], io['x_sample'].rearrange("b s n -> (b s) n")).then_inc(x_in, 16)
            act.wait_ge(c_in, 32)
            run(c_tok[0:NC_, :], c_tok[0:NC_, :], ACT.Silu).then_inc(c_silu, 1)
            for u in range(SPLIT):
                split(u)

            def square(m, n, ready, count):
                act.wait_ge(ready, count)
                if n * KB + m >= 2:
                    act.wait_ge(summed, n * KB + m - 1)
                run(sq[:, m % 2, :], x[:, m, :], ACT.Square).then_inc(squared, 1)

            def rms(n):
                run(warm, eps, ACT.Ln)
                act.wait_ge(ms_ready, n + 1)
                chain(run(ln_ms, psum[:, B_NORM, 0:T], ACT.Ln, bias=eps, scale=1.0 / D))
                run(rstd, ln_ms, ACT.Exp, scale=-0.5).then_inc(rstd_ready, 1)

            def modulate(n, sh, first, end):
                for k in range(first, end):
                    if k % Q == 0:
                        act.wait_ge(samp_ready, n * 4 + k // Q + 1)
                        run(h_hi[:, k:k + Q, SEQ:T], h_samp[:, k:k + Q, :], ACT.Copy).then_inc(samp_hi_ready, 1)
                    act.wait_ge(xn_ready, n * KB + k + 1)
                    run(h_hi[:, k, 0:SEQ], xn[:, k % 3, 0:SEQ], ACT.Identity,
                        bias=mod[:, KB * sh + k, 0:1]).then_inc(h_hi_ready, 1)

            act.wait_ge(set_up, SET_UP)
            for u in range(U_F1):
                finished(u)
                if u % 8 == 7:
                    copy_mod()
                if X_AT < u <= X_AT + KB:
                    k = u - X_AT - 1
                    act.wait_ge(x_turned, k + 1)
                    run(x[:, k, :], bank(k), ACT.Copy).then_inc(dve_freed, 1)
                if X_AT + 1 < u <= X_AT + 1 + KB:
                    square(u - X_AT - 2, 0, dve_freed, u - X_AT - 1)
                if u - 1 in MOD_AT:
                    k = MOD_AT.index(u - 1)
                    modulate(0, 0, k, k + 1)
                split(u + SPLIT)
                if u == 10:
                    act.wait_ge(sp_ready, 1)
                    run(sp_e, sp_e, ACT.Exp, scale=-1.0).then_inc(sp_exp, 1)
                if u == RMS_AT:
                    rms(0)
            modulate(0, 0, 3 * Q, KB)

            def ffn(u0, g0, s0, x0, norm, with_mod):
                def silu(g, step, s_before):
                    run(silu_g[:, step % 2, :], bank(g), ACT.Silu).then_inc(silu_ready, 1)

                def up_pair(u, turns, g, with_group):
                    n = 0
                    for step in range(2):
                        for w in range(2):
                            for half in range(2):
                                if with_group:
                                    finished(u, turns)
                                    split(u + SPLIT, turns)
                                    if n == 7:
                                        copy_mod()
                                    u += 1
                                finished(u, turns)
                                if w == 0 and half == 1:
                                    silu(g, step, s0)
                                split(u + SPLIT, turns)
                                u += 1
                                n += 1
                            g += 1

                def down_eight(u, turns, with_group):
                    for n in range(8):
                        if with_group:
                            for k in range(2):
                                finished(u, turns)
                                if (2 * n + k) % 8 == 7:
                                    copy_mod()
                                split(u + SPLIT, turns)
                                u += 1
                        finished(u, turns)
                        split(u + SPLIT, turns)
                        u += 1

                def chunk(u, turns, g, mod_up, mod_down):
                    per = 2 if mod_up else 1
                    with act.Fori(0, 4) as i:
                        up_pair(u, turns + i * per, g, mod_up)
                    u, g = u + CB * 4 * per, g + 2 * CB
                    per = 3 if mod_down else 1
                    with act.Fori(0, 2) as i:
                        down_eight(u, turns + i * per, mod_down)
                    return u + KB + (2 * KB if mod_down else 0), g + KB

                if with_mod:
                    with act.Fori(0, 3) as c:
                        chunk(u0, c * 14, g0, True, True)
                    u, g = chunk(u0 + 3 * 112, 0, g0 + 3 * CH_G, True, False)
                    u, g = chunk(u, 0, g, False, False)
                else:
                    with act.Fori(0, CHUNKS) as c:
                        chunk(u0, c * 6, g0, False, False)
                    u, g = u0 + CHUNKS * CH_U, g0 + CHUNKS * CH_G
                for s in range(TAIL):
                    for n in range(4):
                        finished(u)
                        if n == 1:
                            silu(g, s, s0)
                        split(u + SPLIT)
                        u += 1
                    g += 2
                for n in range(KB // 2):
                    finished(u)
                    if u + SPLIT < U_END:
                        split(u + SPLIT)
                    for m in range(2):
                        square(2 * n + m, norm, x_done, x0 + CHUNKS * KB + 2 * n + m + 1)
                    u += 1

            ffn(U_F1, G_F1, 0, 0, 1, True)
            rms(1)
            modulate(1, 3, 0, KB)

            def evacuate(n):
                kind, kv, h = MIX_KIND[n]
                src = bank(MIX_GROUP[n])
                head = GRP * kv + h
                if kind in "kq":
                    r = kv if kind == "k" else NKV + head
                    if r:
                        act.wait_ge(rope_done, r)
                    run(swapped[0:64, :], src[64:128, :], ACT.Copy)
                    run(swapped[64:128, :], src[0:64, :], ACT.Copy).then_inc(swapped_ready, 1)
                if kind == "x":
                    if head:
                        act.wait_ge(xc_ready, head)
                    run(xb_p[:, 3:3 + SEQ], src[:, 0:SEQ], ACT.Copy)
                    run(xb_s[:, :, 3:3 + DS], sample(src), ACT.Copy).then_inc(act_freed, 1)
                if kind == "y":
                    if head:
                        act.wait_ge(lru_done, head)
                    run(yf, src, ACT.Copy)
                    run(gel, src, ACT.Square).then_inc(act_freed, 1)

            def gate_functions(kv, h, n):
                head = GRP * kv + h
                act.wait_ge(gates_ready, head + 1)
                if head:
                    act.wait_ge(lru_done, head)
                run(th_r, bank(MIX_GROUP[n] + 1), ACT.Tanh, scale=0.5, bias=half_ba[:, head:head + 1]).then_inc(act_freed, 1)
                run(th_x, bank(MIX_GROUP[n] + 2), ACT.Tanh, scale=0.5, bias=half_bx[:, head:head + 1]).then_inc(act_freed, 1)
                act.wait_ge(act_freed, 4 * head + 4)
                m4, m2 = m4sp[:, head:head + 1], m2sp[:, head:head + 1]
                run(a_p, th_r[:, 0:SEQ], ACT.Exp, scale=m4, bias=m4)
                run(a_s[:, :, 1:1 + DS], sample(th_r), ACT.Exp, scale=m4, bias=m4)
                chain(run(root, th_r, ACT.Tanh, scale=m2, bias=m2))
                run(root, root, ACT.Sqrt, scale=-0.25).then_inc(gate_acts, 1)

            def gelu_tanh(head):
                act.wait_ge(gel_z, head + 1)
                run(gel, gel, ACT.Tanh, scale=GELU_C).then_inc(gel_t, 1)

            def copy_cached_keys(kv, half):
                act.wait_ge(ck_turned, 2 * kv + half + 1)
                run(ck_t[:, 4 * half:4 * half + 4, :], psum[:, B_PT, :].rearrange("p (b n) -> p b n", n=P),
                    ACT.Copy).then_inc(ck_ready, 1)

            def copy_probs(kv, t):
                act.wait_ge(pt_turned, 6 * kv + t + 1)
                if t < GRP:
                    run(probs_t, psum[:, B_PT, 0:3 * P], ACT.Copy).then_inc(pt_copied, 1)
                else:
                    run(probs_t[:, 0:P], psum[:, B_PT, 0:P], ACT.Copy)
                    run(probs_t[0:SAMP, P:2 * P], psum[0:SAMP, B_PT, P:2 * P], ACT.Copy).then_inc(pt_copied, 1)

            def copy_values(kv, t):
                act.wait_ge(o_ready, 6 * kv + t + 1)
                if t < GRP:
                    run(mix[:, LH + GRP * kv + t, 0:SEQ], psum[:, B_O, 0:SEQ], ACT.Copy).then_inc(o_copied, 1)
                else:
                    for g in range(GRP):
                        src = psum[:, B_O, 0:P].rearrange("p (b g s) -> p g b s", g=GRP, s=DS)[:, g]
                        dst = mix[:, LH + GRP * kv + g, SEQ + 32 * (t - GRP):SEQ + 32 * (t - GRP + 1)]
                        last = run(dst.rearrange("p (b s) -> p b s", s=DS), src, ACT.Copy)
                    last.then_inc(o_copied, 1)

            def exponents(kv, t):
                act.wait_ge(maxed, 6 * kv + t + 1)
                if t < GRP:
                    head = GRP * kv + t
                    run(score[:, 0:P], score[:, 0:P], ACT.Exp, bias=neg_top[:, 0:1], accum_out=den[:, 0:1])
                    run(score[:, P:3 * P], score[:, P:3 * P], ACT.Exp, bias=neg_top[:, 1:2], accum_out=den[:, 1:2])
                    run(sink_e[:, 0:2], neg_top[:, 0:2], ACT.Exp, bias=sinks[:, head:head + 1]).then_inc(exp_done, 1)
                else:
                    run(score[:, 0:P + SAMP], score[:, 0:P + SAMP], ACT.Exp, bias=neg_top[:, 0:1], accum_out=den[:, 0:1])
                    run(sink_e[:, 0:1], neg_top[:, 0:1], ACT.Exp, bias=sink_s[:, kv:kv + 1]).then_inc(exp_done, 1)

            def attended(kv, t):
                if t >= 2:
                    copy_values(kv, t - 2)
                if 1 <= t <= 6:
                    copy_probs(kv, t - 1)
                if t < 6:
                    exponents(kv, t)

            def behind(n):
                kind, kv, h = MIX_KIND[n]
                if kind == "q" and h < 2:
                    copy_cached_keys(kv, h)
                if kind == "x":
                    attended(kv, 2 * h)
                if kind == "y":
                    attended(kv, 2 * h + 1)
                    gelu_tanh(GRP * kv + h)
                    gate_functions(kv, h, n)

            for n in range(MIX_BLOCKS):
                if n:
                    behind(n - 1)
                for half in range(2):
                    finished(U_MIX + 2 * n + half)
                    if half:
                        evacuate(n)
                    split(U_MIX + 2 * n + half + SPLIT)
            behind(MIX_BLOCKS - 1)

            for k in [*range(LH, KB), *range(LH)]:
                if k < LH:
                    act.wait_ge(lru_done, k + 1)
                if k == LH:
                    act.wait_ge(o_copied, 12)
                run(h_hi[:, k, :], mix[:, k, :], ACT.Copy).then_inc(h_hi_ready, 1)
            act.wait_ge(tok_stored, TOK_DMAS * 16)
            with act.Fori(0, 4) as i:
                for n in range(8):
                    finished(U_OUT + n, i)
                    split(U_OUT + n + SPLIT, i)
                    if n % 2:
                        act.wait_ge(x_done, i * 4 + X_OUT + n // 2 + 1)
                        act.wait_ge(summed, i * 4 + 2 * KB + n // 2 - 1)
                        run(sq[:, n // 2 % 2, :], x[:, bass.ds(i * 4 + n // 2, 1), :].rearrange("p a n -> p (a n)"),
                            ACT.Square).then_inc(squared, 1)

            rms(2)
            modulate(2, 6, 0, KB)
            act.wait_ge(st_turned, 1)
            run(prm[:, 0:2 * P], psum[:, B_SCORE, 0:2 * P], ACT.Copy)
            run(prm[0:32, 2 * P:3 * P], psum[0:32, B_SCORE, 2 * P:3 * P], ACT.Copy).then_inc(st_copied, 1)
            ffn(U_F2, G_F2, FB, X_F2, 3, False)
            rms(3)
            for k in range(KB):
                act.wait_ge(y_turned, k + 1)
                src = psum[:, 4 + k % 2, :]
                run(y_tok[:, 0:2, k * P:(k + 1) * P], src[:, 0:2 * P].rearrange("p (t n) -> p t n", n=P), ACT.Copy)
                run(y_tok[0:SAMP, 2, k * P:(k + 1) * P], src[0:SAMP, 2 * P:3 * P], ACT.Copy).then_inc(y_copied, 1)

        @block.vector
        def _(dve):
            v = nc.vector
            chained = [0]

            def chain(instruction):
                chained[0] += 1
                instruction.then_inc(dve_chain, 1)
                dve.wait_ge(dve_chain, chained[0])

            def split(u, turns=None):
                n = unit_floats(u)
                dve.wait_ge(hi_done, plus(u + 1, turns, RAW))
                v.tensor_tensor(lo_slot(u)[:, 0:n], raw_slot(u)[:, 0:n], hi_slot(u)[:, 0:n],
                                ALU.subtract).then_inc(lo_done, 1)

            def finished(u, turns=None):
                dve.wait_ge(unit_done, plus(u + 1, turns, RAW))

            def add_mod(group, place=None):
                place = group if place is None else place
                at = mod[:, bass.ds(place * 4, 4), :]
                src = psum[:, B_MODT, :].rearrange("p (j c) -> p j c", c=P)
                bias = prm[:, bass.ds(place * 4 + C_ADAB, 4)].unsqueeze(2).broadcast_to((P, 4, NC_))
                dve.wait_ge(mod_turned, group + 1)
                v.tensor_tensor(at, src[:, :, 0:NC_], bias, ALU.add).then_inc(mod_half, 1)
                dve.wait_ge(mod_half, group + 1)
                v.tensor_tensor(at, at, src[:, :, NC_:2 * NC_], ALU.add).then_inc(mod_done, 1)

            for u in range(SPLIT):
                split(u)
            dve.wait_ge(c_turned, 1)
            src = psum[:, 5, 0:NC_ * KB].rearrange("p (k c) -> p k c", c=NC_)
            chain(v.tensor_copy(c_split[:, :, 0:NC_], src))
            v.tensor_tensor(c_split[:, :, NC_:2 * NC_], src, c_split[:, :, 0:NC_], ALU.subtract).then_inc(c_ready, 1)
            def scale(n, vector, k0, blocks, groups):
                at = mod[:, KB * vector + k0:KB * vector + k0 + blocks, :]
                w = prm[:, C_NORM + KB * n + k0:C_NORM + KB * n + k0 + blocks].unsqueeze(2).broadcast_to((P, blocks, NC_))
                dve.wait_ge(mod_done, groups)
                v.scalar_tensor_tensor(out=at, in0=at, scalar=1.0, in1=w, op0=ALU.add, op1=ALU.mult).then_inc(scale_ready, 1)

            def normed(n, sc, k):
                dve.wait_ge(rstd_ready, n + 1)
                dve.wait_ge(scale_ready, k // Q + 1 if n == 0 else 4 + n)
                if k >= 3:
                    dve.wait_ge(h_ready, H_BASE[n] + k - 2)
                v.scalar_tensor_tensor(out=xn[:, k % 3, 0:SEQ], in0=x[:, k, 0:SEQ], scalar=mod[:, KB * sc + k, 0:1],
                                       in1=rstd[:, 0:SEQ], op0=ALU.mult, op1=ALU.mult).then_inc(xn_ready, 1)

            def lo_part(n, sh, k):
                if k % Q == 0:
                    dve.wait_ge(samp_hi_ready, n * 4 + k // Q + 1)
                    v.tensor_tensor(h_lo[:, k:k + Q, SEQ:T], h_samp[:, k:k + Q, :], h_hi[:, k:k + Q, SEQ:T],
                                    ALU.subtract).then_inc(samp_lo_ready, 1)
                    dve.wait_ge(samp_lo_ready, n * 4 + k // Q + 1)
                dve.wait_ge(h_hi_ready, H_BASE[n] + k + 1)
                v.scalar_tensor_tensor(out=h_lo[:, k, 0:SEQ], in0=xn[:, k % 3, 0:SEQ], scalar=mod[:, KB * sh + k, 0:1],
                                       in1=h_hi[:, k, 0:SEQ], op0=ALU.add, op1=ALU.subtract).then_inc(h_ready, 1)

            def modulate(n, sc, sh, first, end):
                for k in range(first, end + 2):
                    if k < end:
                        normed(n, sc, k)
                    if k - 2 >= first:
                        lo_part(n, sh, k - 2)

            def parameters():
                dve.wait_ge(prm_turned, 1)
                v.tensor_copy(prm[:, 0:2 * P], psum[:, B_NORM, 0:2 * P])
                v.tensor_copy(prm[:, 2 * P:2 * P + 16], psum[:, B_MODT, 0:16])
                v.tensor_copy(prm[:, C_SCONV:N_PRM], psum[:, B_NORM, 2 * P:4 * P]).then_inc(prm_ready, 1)
                dve.wait_ge(prm_ready, 1)

            def lru_constants():
                lam = prm[:, C_LAM:C_LAM + LH]
                chain(v.tensor_scalar(sp_s, lam, -1.0, None, ALU.mult))
                v.tensor_tensor(sp_e, lam, sp_s, ALU.max).then_inc(sp_ready, 1)
                dve.wait_ge(sp_exp, 1)
                chain(v.tensor_scalar(sp_q, sp_e, 2.0, None, ALU.add))
                chain(v.reciprocal(sp_q, sp_q))
                chain(v.tensor_tensor(sp_e, sp_e, sp_q, ALU.mult))
                chain(v.tensor_tensor(sp_s, sp_e, sp_e, ALU.mult))
                chain(v.tensor_scalar(sp_q, sp_s, 1.0 / 15, None, ALU.mult))
                for odd in (13, 11, 9, 7, 5, 3):
                    chain(v.scalar_tensor_tensor(out=sp_q, in0=sp_q, scalar=1.0 / odd, in1=sp_s, op0=ALU.add, op1=ALU.mult))
                chain(v.scalar_tensor_tensor(out=sp_q, in0=sp_q, scalar=1.0, in1=sp_e, op0=ALU.add, op1=ALU.mult))
                chain(v.tensor_scalar(sp_s, lam, -1.0, 0.0, ALU.mult, ALU.max))
                chain(v.scalar_tensor_tensor(out=sp_s, in0=sp_q, scalar=2.0, in1=sp_s, op0=ALU.mult, op1=ALU.add))
                v.tensor_scalar(m2sp, sp_s, -2.0, None, ALU.mult)
                v.tensor_scalar(m4sp, sp_s, -4.0, None, ALU.mult)
                v.tensor_scalar(half_ba, prm[:, C_BA:C_BA + LH], 0.5, None, ALU.mult)
                v.tensor_scalar(half_bx, prm[:, C_BX:C_BX + LH], 0.5, None, ALU.mult)
                v.tensor_copy(final_norm, prm[:, C_NORM + 3 * KB:C_NORM + 4 * KB])
            for u in range(U_F1):
                finished(u)
                if u % 8 == 7:
                    group = u // 8
                    if group == 0:
                        parameters()
                    add_mod(group, group // 2 + group % 2 * Q)
                    if group % 2:
                        scale(0, 1, group // 2 * Q, Q, group + 1)
                if u - 2 in MOD_AT:
                    lo_part(0, 0, MOD_AT.index(u - 2))
                if u in MOD_AT:
                    normed(0, 1, MOD_AT.index(u))
                split(u + SPLIT)
                if u == 8:
                    lru_constants()
            modulate(0, 1, 0, 3 * Q, KB)

            def update(m, g, vector, before):
                gate = mod[:, bass.ds(m + KB * vector, 1), :].rearrange("p a c -> p (a c)")
                xm = x[:, bass.ds(m, 1), :].rearrange("p a n -> p (a n)")
                src = bank(g)
                v.scalar_tensor_tensor(out=xm[:, 0:SEQ], in0=src[:, 0:SEQ], scalar=gate[:, 0:1], in1=xm[:, 0:SEQ],
                                       op0=ALU.mult, op1=ALU.add)
                v.tensor_tensor(sample(prod[:, g % 2, :]), sample(src), gate[:, 1:NC_].unsqueeze(2).broadcast_to((P, NB, DS)),
                                ALU.mult).then_inc(dve_freed, 1)
                dve.wait_ge(dve_freed, before + 1)
                v.tensor_tensor(xm[:, SEQ:T], xm[:, SEQ:T], prod[:, g % 2, SEQ:T], ALU.add).then_inc(x_done, 1)

            def ffn(u0, g0, a0, vector, freed_before, with_mod):
                def hidden(step, g, gturns, block_of, count):
                    dve.wait_ge(silu_ready, count + 1)
                    v.scalar_tensor_tensor(out=prod[:, step % 2, :], in0=silu_g[:, step % 2, :], scalar=0.5,
                                           in1=bank(g + 1), op0=ALU.mult, op1=ALU.mult).then_inc(dve_freed, 2)
                    dve.wait_ge(dve_freed, plus(g + 2 - freed_before, gturns, ACC))
                    dst_hi = a_hi[:, bass.ds(block_of, 1), :].rearrange("p a n -> p (a n)")
                    dst_lo = a_lo[:, bass.ds(block_of, 1), :].rearrange("p a n -> p (a n)")
                    v.tensor_copy(dst_hi, prod[:, step % 2, :]).then_inc(a_hi_ready, 1)
                    dve.wait_ge(a_hi_ready, count + 1)
                    v.tensor_tensor(dst_lo, prod[:, step % 2, :], dst_hi, ALU.subtract).then_inc(a_ready, 1)

                def up_pair(u, turns, g, gturns, first_block, count, group):
                    n = 0
                    for step in range(2):
                        for w in range(2):
                            for half in range(2):
                                if group is not None:
                                    finished(u, turns)
                                    split(u + SPLIT, turns)
                                    u += 1
                                finished(u, turns)
                                if w == 1 and half == 1:
                                    hidden(step, g, gturns, first_block + step, count + step)
                                    g += 2
                                    if group is not None and step == 1:
                                        add_mod(group)
                                split(u + SPLIT, turns)
                                u += 1
                                n += 1

                def down_eight(u, turns, g, gturns, m, group):
                    for n in range(8):
                        if group is not None:
                            for k in range(2):
                                finished(u, turns)
                                split(u + SPLIT, turns)
                                u += 1
                        finished(u, turns)
                        update(m + n, g, vector, plus(g - freed_before, gturns, ACC))
                        g += 1
                        if group is not None and n % 4 == 3:
                            add_mod(group + n // 4)
                        split(u + SPLIT, turns)
                        u += 1

                def chunk(u, turns, g, gturns, count, group, mod_up, mod_down):
                    per = 2 if mod_up else 1
                    with dve.Fori(0, 4) as i:
                        up_pair(u, turns + i * per, g, gturns + i, i * 2, count + i * 2, group + i if mod_up else None)
                    u, g = u + CB * 4 * per, g + 2 * CB
                    per = 3 if mod_down else 1
                    dve.wait_ge(mod_done, 4 * (vector + 1))
                    with dve.Fori(0, 2) as i:
                        down_eight(u, turns + i * per, g, gturns + i * 2, i * 8, group + 4 + i * 2 if mod_down else None)
                    return u + KB + (2 * KB if mod_down else 0), g + KB

                if with_mod:
                    with dve.Fori(0, 3) as c:
                        chunk(u0, c * 14, g0, c * 8, c * CB + a0, c * 8 + 8, True, True)
                    u, g = chunk(u0 + 3 * 112, 0, g0 + 3 * CH_G, 0, a0 + 3 * CB, 32, True, False)
                    scale(1, 4, 0, KB, 36)
                    scale(2, 7, 0, KB, 36)
                    u, g = chunk(u, 0, g, 0, a0 + 4 * CB, 0, False, False)
                else:
                    with dve.Fori(0, CHUNKS) as c:
                        chunk(u0, c * 6, g0, c * 8, c * CB + a0, 0, False, False)
                    u, g = u0 + CHUNKS * CH_U, g0 + CHUNKS * CH_G
                for s in range(TAIL):
                    for n in range(4):
                        finished(u)
                        if n == 3:
                            hidden(s, g, None, s, a0 + CHUNKS * CB + s)
                        split(u + SPLIT)
                        u += 1
                    g += 2
                for n in range(KB // 2):
                    finished(u)
                    for m in range(2):
                        update(2 * n + m, g, vector, g - freed_before)
                        g += 1
                    if u + SPLIT < U_END:
                        split(u + SPLIT)
                    u += 1

            ffn(U_F1, G_F1, 0, 2, 0, True)
            dve.wait_ge(sinks_in, 16)
            dve.wait_ge(tables_in, 16)
            for kv in range(NKV):
                chain(v.tensor_tensor(sink_pick, sinks[:, GRP * kv:GRP * (kv + 1)], group_of, ALU.mult))
                chain(v.reduce_sum(sink_s[:, kv:kv + 1], sink_pick, AX.X))

            modulate(1, 4, 3, 0, KB)

            def evacuate(n):
                kind, kv, h = MIX_KIND[n]
                src = bank(MIX_GROUP[n])
                if kind == "v":
                    v.tensor_copy(v_t[:, kv, :], src).then_inc(dve_freed, 1)
                if kind in "kq":
                    r = kv if kind == "k" else NKV + GRP * kv + h
                    dve.wait_ge(swapped_ready, r + 1)
                    v.tensor_tensor(rope_c, src, cos, ALU.mult)
                    v.tensor_tensor(rope_s, swapped, sin, ALU.mult).then_inc(dve_freed, 1)
                    dve.wait_ge(dve_freed, MIX_FREED[MIX_GROUP[n] - G_MIX][1])
                    if kind == "k":
                        v.tensor_tensor(k_t[:, kv, :], rope_c, rope_s, ALU.add).then_inc(rope_done, 1)
                    else:
                        v.tensor_tensor(q_p[:, h, :], rope_c[:, 0:SEQ], rope_s[:, 0:SEQ], ALU.add)
                        v.tensor_tensor(q_s[:, :, h, :], sample(rope_c), sample(rope_s), ALU.add).then_inc(rope_done, 1)

            conv_state = prm[:, C_SCONV:C_SCONV + NB * 3 * LH].rearrange("p (b j k) -> p b j k", j=3, k=LH)
            new_conv_s = st[:, 0:192].rearrange("p (b j k) -> p b j k", j=3, k=LH)
            new_conv_p = st[:, 256:280].rearrange("p (j k) -> p j k", k=LH)

            def convolve(head):
                xc = xc2[:, head % 2, :]
                if head > 1:
                    dve.wait_ge(gates_ready, head - 1)
                    dve.wait_ge(lru_done, head - 1)
                dve.wait_ge(xb_state, head + 2)
                dve.wait_ge(act_freed, 4 * head + 1)
                w = [prm[:, C_CW + j * LH + head:C_CW + j * LH + head + 1] for j in range(CONV)]
                b = prm[:, C_CB + head:C_CB + head + 1]
                v.tensor_copy(new_conv_s[:, :, :, head], xb_s[:, :, DS:DS + 3])
                v.tensor_copy(new_conv_p[:, :, head], xb_p[:, SEQ:SEQ + 3])
                v.tensor_scalar(xc[:, 0:SEQ], xb_p[:, 0:SEQ], w[0], b, ALU.mult, ALU.add)
                chain(v.tensor_scalar(sample(xc), xb_s[:, :, 0:DS], w[0], b, ALU.mult, ALU.add))
                for j in range(1, CONV):
                    v.scalar_tensor_tensor(out=xc[:, 0:SEQ], in0=xb_p[:, j:j + SEQ], scalar=w[j], in1=xc[:, 0:SEQ],
                                           op0=ALU.mult, op1=ALU.add)
                    last = v.scalar_tensor_tensor(out=sample(xc), in0=xb_s[:, :, j:j + DS], scalar=w[j], in1=sample(xc),
                                                  op0=ALU.mult, op1=ALU.add)
                    if j < CONV - 1:
                        chain(last)
                last.then_inc(xc_ready, 1)

            def recurrence(head):
                dve.wait_ge(gate_acts, head + 1)
                v.scalar_tensor_tensor(out=root[:, 0:SEQ], in0=a_p, scalar=1.0, in1=root[:, 0:SEQ], op0=ALU.add, op1=ALU.mult)
                chain(v.scalar_tensor_tensor(out=sample(root), in0=a_s[:, :, 1:1 + DS], scalar=1.0, in1=sample(root),
                                             op0=ALU.add, op1=ALU.mult))
                chain(v.scalar_tensor_tensor(out=root, in0=th_x, scalar=1.0, in1=root, op0=ALU.add, op1=ALU.mult))
                xc = xc2[:, head % 2, :]
                dve.wait_ge(xc_ready, head + 1)
                v.tensor_tensor(u_p, root[:, 0:SEQ], xc[:, 0:SEQ], ALU.mult)
                v.tensor_copy(u_s[:, :, 0], prm[:, C_SLRU:C_SLRU + NB * LH].rearrange("p (b k) -> p b k", k=LH)[:, :, head])
                chain(v.tensor_tensor(u_s[:, :, 1:1 + DS], sample(root), sample(xc), ALU.mult))
                if head:
                    dve.wait_ge(state_saved, head)
                v.tensor_tensor_scan(hs_p, a_p, u_p, 0.0, ALU.mult, ALU.add)
                chain(v.tensor_tensor_scan(hs_s.rearrange("p b s -> p (b s)"), a_s.rearrange("p b s -> p (b s)"),
                                           u_s.rearrange("p b s -> p (b s)"), 0.0, ALU.mult, ALU.add))
                dve.wait_ge(gelu_ready, head + 1)
                v.scalar_tensor_tensor(out=mix[:, head, 0:SEQ], in0=gel[:, 0:SEQ], scalar=0.5, in1=hs_p,
                                       op0=ALU.mult, op1=ALU.mult)
                v.scalar_tensor_tensor(out=sample(mix[:, head, :]), in0=sample(gel), scalar=0.5, in1=hs_s[:, :, 1:1 + DS],
                                       op0=ALU.mult, op1=ALU.mult).then_inc(lru_done, 1)

            def copy_tokens(kv):
                dve.wait_ge(tok_turned, kv + 1)
                src = psum[:, B_TOK, :]
                v.tensor_copy(tok[:, 0, kv, :], src[:, 0:P])
                v.tensor_copy(tok[:, 1, kv, :], src[:, P:2 * P])
                v.tensor_copy(tok[:, 3, kv, :], src[:, 2 * P:3 * P])
                v.tensor_copy(tok[0:SAMP, 2, kv, :], src[0:SAMP, 3 * P:4 * P])
                v.tensor_copy(tok[0:SAMP, 4, kv, :], psum[0:SAMP, B_O, 0:P]).then_inc(tok_ready, 1)

            def softmax_head(kv, t):
                job = 6 * kv + t
                dve.wait_ge(scored, job + 1)
                n, mask = (3 * P, mask_p) if t < GRP else (P + SAMP, mask_s[t - GRP])
                v.scalar_tensor_tensor(out=score[:, 0:n], in0=psum[:, B_SCORE, 0:n], scalar=SCALE, in1=mask,
                                       op0=ALU.mult, op1=ALU.add).then_inc(masked, 1)
                dve.wait_ge(masked, job + 1)
                if t < GRP:
                    v.reduce_max(top[:, 0:1], score[:, 0:P], AX.X)
                    chain(v.reduce_max(top[:, 1:2], score[:, P:3 * P], AX.X))
                    head = GRP * kv + t
                    v.tensor_scalar(neg_top, top, sinks[:, head:head + 1], -1.0, ALU.max, ALU.mult).then_inc(maxed, 1)
                else:
                    chain(v.reduce_max(top[:, 0:1], score[:, 0:n], AX.X))
                    v.tensor_scalar(neg_top[:, 0:1], top[:, 0:1], sink_s[:, kv:kv + 1], -1.0, ALU.max,
                                    ALU.mult).then_inc(maxed, 1)

            def softmax_tail(kv, t):
                job = 6 * kv + t
                dve.wait_ge(exp_done, job + 1)
                m = 2 if t < GRP else 1
                chain(v.tensor_tensor(den[:, 0:m], den[:, 0:m], sink_e[:, 0:m], ALU.add))
                chain(v.reciprocal(den[:, 0:m], den[:, 0:m]))
                if t < GRP:
                    v.tensor_scalar(score[:, 0:P], score[:, 0:P], den[:, 0:1], None, ALU.mult)
                    v.tensor_scalar(score[:, P:3 * P], score[:, P:3 * P], den[:, 1:2], None, ALU.mult).then_inc(probs_ready, 1)
                else:
                    v.tensor_scalar(score[:, 0:P + SAMP], score[:, 0:P + SAMP], den[:, 0:1], None,
                                    ALU.mult).then_inc(probs_ready, 1)

            def behind(n):
                kind, kv, h = MIX_KIND[n]
                if kind == "q" and h < 2 and kv == 0:
                    copy_tokens(h)
                t = 2 * h + (kind == "y")
                attends = kind in ("x", "y") and t < 6
                if attends:
                    softmax_head(kv, t)
                if kind == "x":
                    convolve(GRP * kv + h)
                if attends:
                    softmax_tail(kv, t)
                if kind == "y":
                    recurrence(GRP * kv + h)

            for n in range(MIX_BLOCKS):
                if n:
                    behind(n - 1)
                finished(U_MIX + 2 * n)
                split(U_MIX + 2 * n + SPLIT)
                finished(U_MIX + 2 * n + 1)
                evacuate(n)
                split(U_MIX + 2 * n + 1 + SPLIT)
            behind(MIX_BLOCKS - 1)

            for i, k in enumerate([*range(LH, KB), *range(LH)]):
                dve.wait_ge(h_hi_ready, 2 * KB + i + 1)
                v.tensor_tensor(h_lo[:, k, :], mix[:, k, :], h_hi[:, k, :], ALU.subtract).then_inc(h_ready, 1)
            with dve.Fori(0, 4) as i:
                for n in range(8):
                    finished(U_OUT + n, i)
                    if n % 2:
                        update(i * 4 + n // 2, G_OUT + n // 2, 5, plus(G_OUT + n // 2 - ACT_FREED, i, ACC))
                    split(U_OUT + n + SPLIT, i)
            modulate(2, 7, 6, 0, KB)
            ffn(U_F2, G_F2, FB, 8, ACT_FREED, False)

            dve.wait_ge(rstd_ready, 4)
            for k in range(KB):
                if k >= 3:
                    dve.wait_ge(y_turned, k - 2)
                v.scalar_tensor_tensor(out=xn[:, k % 3, :], in0=x[:, k, :], scalar=final_norm[:, k:k + 1], in1=rstd,
                                       op0=ALU.mult, op1=ALU.mult).then_inc(xn_y, 1)

        @block.gpsimd
        def _(pool):
            g = nc.gpsimd
            chained = [0]

            def chain(instruction):
                chained[0] += 1
                instruction.then_inc(pool_chain, 1)
                pool.wait_ge(pool_chain, chained[0])

            g.memset(ones, 1.0).then_inc(set_up, 1)
            g.memset(eps, EPS).then_inc(set_up, 1)
            g.memset(mod_row, 0.0).then_inc(set_up, 1)
            g.memset(a_s[:, :, 0:1], 0.0)
            row = 0
            for name in ('norm_ffn1', 'norm_mix', 'norm_ffn2'):
                pool.dma_start(prm_tok[row:row + KB, 0, :], io[name].rearrange("a (k n) -> (a k) n", n=P)).then_inc(prm_in, 16)
                row += KB
            pool.dma_start(prm_tok[row:row + KB, 0, :], io['norm_final'].rearrange("(k n) -> k n", n=P)).then_inc(prm_in, 16)
            row += KB
            pool.dma_start(prm_tok[row:row + 32, 0, :], io['conv_w'][0].rearrange("j (k n) -> (j k) n", n=P)).then_inc(prm_in, 16)
            row += 32
            pool.dma_start(prm_tok[row:row + 8, 0, :], io['conv_b'].rearrange("a (k n) -> (a k) n", n=P)).then_inc(prm_in, 16)
            pool.dma_start(prm_tok[row + 8:row + 16, 0, :], io['lru_b_a'][0]).then_inc(prm_in, 16)
            pool.dma_start(prm_tok[row + 16:row + 24, 0, :], io['lru_b_x'][0]).then_inc(prm_in, 16)
            pool.dma_start(prm_tok[row + 24:row + 32, 0, :], io['lru_lambda'].rearrange("a (k n) -> (a k) n", n=P)).then_inc(prm_in, 16)
            ada_b = io['ada_b'].rearrange("a (k n) -> (a k) n", n=P)
            pool.dma_start(prm_tok[:, 1, :], ada_b[0:P]).then_inc(prm_in, 16)
            pool.dma_start(prm_tok[0:16, 4, :], ada_b[P:P + 16]).then_inc(prm_in, 16)
            conv = io['state_conv'][0].rearrange("b j (k n) -> (b j k) n", n=P)
            pool.dma_start(prm_tok[:, 2, :], conv[0:P]).then_inc(prm_in, 16)
            pool.dma_start(prm_tok[0:64, 3, :], conv[P:192]).then_inc(prm_in, 16)
            pool.dma_start(prm_tok[64:128, 3, :], io['state_lru'][0].rearrange("b (k n) -> (b k) n", n=P)).then_inc(prm_in, 16)

            def load_cached_keys(kv):
                src = io['cache_k_win'][0, :, :, kv, :].rearrange("b s d -> s b d")
                pool.dma_start(ck_tok, src).then_inc(ck_in, 16)

            def load_cached_values(kv):
                src = io['cache_v_win'][0, :, :, kv, :].rearrange("b s d -> s b d")
                pool.dma_start(cv_tok, src).then_inc(cv_in, 16)

            def load_gates(kv):
                heads = slice(GRP * kv, GRP * (kv + 1))
                pool.dma_start(w_a, io['lru_w_a'][0, heads].rearrange("h i j -> i h j")).then_inc(gates_in, 16)
                pool.dma_start(w_x, io['lru_w_x'][0, heads].rearrange("h i j -> i h j")).then_inc(gates_in, 16)

            def add_squares(n):
                for m in range(KB):
                    pool.wait_ge(squared, n * KB + m + 1)
                    if m == 0:
                        if n:
                            pool.wait_ge(ms_ready, n)
                        g.tensor_copy(sum_sq, sq[:, 0, :]).then_inc(summed, 1)
                    else:
                        pool.wait_ge(summed, n * KB + m)
                        g.tensor_tensor(sum_sq, sum_sq, sq[:, m % 2, :], ALU.add).then_inc(summed, 1)

            def samples(n, sc, sh):
                vec = (lambda at, k: mod[:, KB * at + k:KB * at + k + Q, 1:NC_].unsqueeze(3).broadcast_to((P, Q, NB, DS)))
                for q in range(4):
                    pool.wait_ge(scale_ready, q + 1 if n == 0 else 4 + n)
                    k = q * Q
                    out = h_samp[:, k:k + Q, :].rearrange("p k (b s) -> p k b s", s=DS)
                    chain(g.tensor_tensor(out, x[:, k:k + Q, SEQ:T].rearrange("p k (b s) -> p k b s", s=DS), vec(sc, k),
                                          ALU.mult))
                    if q == 0:
                        pool.wait_ge(rstd_ready, n + 1)
                    chain(g.tensor_tensor(h_samp[:, k:k + Q, :], h_samp[:, k:k + Q, :],
                                          rstd[:, SEQ:T].unsqueeze(1).broadcast_to((P, Q, SAMP)), ALU.mult))
                    g.tensor_tensor(out, out, vec(sh, k), ALU.add).then_inc(samp_ready, 1)

            add_squares(0)
            samples(0, 1, 0)
            pool.wait_ge(unit_done, U_F1)
            pool.dma_start(sinks, io['attn_sinks'].broadcast_to((P, NH))).then_inc(sinks_in, 16)
            pool.dma_start(tables, io['tables']).then_inc(tables_in, 16)
            load_cached_keys(0)
            load_cached_values(0)
            load_gates(0)
            for new, old in (('k_sample', 'cache_k_win'), ('v_sample', 'cache_v_win')):
                pool.dma_start(io[new][0, :, 0:WIN - DS].rearrange("b s h d -> b (s h d)"),
                               io[old][0, :, DS:WIN].rearrange("b s h d -> b (s h d)")).then_inc(cache_stored, 16)

            add_squares(1)
            samples(1, 4, 3)

            conv_state = prm[:, C_SCONV:C_SCONV + NB * 3 * LH].rearrange("p (b j k) -> p b j k", j=3, k=LH)
            new_lru_s = st[:, 192:256].rearrange("p (b k) -> p b k", k=LH)
            new_lru_p = st[:, 280:288]

            def old_state(head):
                if head == 0:
                    pool.wait_ge(tok_turned, NKV)
                    g.memset(xb_p[:, 0:3], 0.0).then_inc(xb_state, 1)
                else:
                    pool.wait_ge(xc_ready, head)
                g.tensor_copy(xb_s[:, :, 0:3], conv_state[:, :, :, head]).then_inc(xb_state, 1)

            def save_state(head):
                pool.wait_ge(lru_done, head + 1)
                g.tensor_copy(new_lru_s[:, :, head], hs_s[:, :, DS])
                g.tensor_copy(new_lru_p[:, head:head + 1], hs_p[:, SEQ - 1:SEQ]).then_inc(state_saved, 1)

            for head in range(LH):
                old_state(head)
                if head == 1:
                    pool.wait_ge(ck_turned, 2)
                    load_cached_keys(1)
                pool.wait_ge(act_freed, 4 * head + 2)
                chain(g.tensor_scalar(gel, gel, 0.044715, 1.0, ALU.mult, ALU.add))
                g.tensor_tensor(gel, gel, yf, ALU.mult).then_inc(gel_z, 1)
                pool.wait_ge(gel_t, head + 1)
                chain(g.tensor_scalar(gel, gel, 1.0, None, ALU.add))
                g.tensor_tensor(gel, gel, yf, ALU.mult).then_inc(gelu_ready, 1)
                if head:
                    save_state(head - 1)
                if head == GRP - 1:
                    pool.wait_ge(gates_ready, GRP)
                    load_gates(1)
                    pool.wait_ge(o_ready, 6)
                    load_cached_values(1)
            save_state(LH - 1)
            pool.wait_ge(tok_stored, TOK_DMAS * 16)
            add_squares(2)
            samples(2, 7, 6)

            pool.wait_ge(st_copied, 1)
            conv_rows = io['conv_sample'][0].rearrange("b j (k n) -> (b j k) n", n=P)
            pool.dma_start(conv_rows[0:P], prm[:, 0:P]).then_inc(state_stored, 16)
            pool.dma_start(conv_rows[P:192], prm[0:64, P:2 * P]).then_inc(state_stored, 16)
            pool.dma_start(io['lru_sample'][0].rearrange("b (k n) -> (b k) n", n=P), prm[64:P, P:2 * P]).then_inc(state_stored, 16)
            pool.dma_start(io['conv_prompt'][0, 0].rearrange("j (k n) -> (j k) n", n=P), prm[0:24, 2 * P:3 * P]).then_inc(state_stored, 16)
            pool.dma_start(io['lru_prompt'][0].rearrange("a (k n) -> (a k) n", n=P), prm[24:32, 2 * P:3 * P]).then_inc(state_stored, 16)
            add_squares(3)


def shape_constants(np):
    i, j = np.arange(P)[:, None], np.arange(2 * P)[None, :]
    never = np.float32(-1e30)
    t = np.zeros((P, 6 * P + 4 + 2 * T), np.float32)
    t[:, 0:P] = np.where(j[:, :P] <= i, 0, never)
    t[:, P:3 * P] = np.where((j <= P + i) & (j >= i), 0, never)
    step, seq = i % DS, i // (GRP * DS)
    new = np.arange(SAMP)[None, :]
    for half in range(2):
        m = t[:, 3 * P + (P + SAMP) * half:3 * P + (P + SAMP) * (half + 1)]
        m[:, 0:P] = np.where(j[:, :P] >= step, 0, never)
        m[:, P:] = np.where((new // DS == 4 * half + seq) & (new % DS <= step), 0, never)
    t[:, 6 * P:6 * P + 4] = (i // DS % GRP == np.arange(GRP)[None, :])
    pos = np.concatenate([np.arange(SEQ), np.tile(PAST + np.arange(DS), NB)]).astype(np.float32)
    inv = (np.float32(10000.0) ** (-np.arange(64, dtype=np.float32) / np.float32(64))).astype(np.float32)
    ang = inv[:, None] * pos[None, :]
    c, s = np.cos(ang), np.sin(ang)
    t[:, 6 * P + 4:6 * P + 4 + T] = np.concatenate([c, c])
    t[:, 6 * P + 4 + T:] = np.concatenate([-s, s])
    return {'identity': np.eye(P, dtype=np.float32), 'tables': t}


def kernel(**inputs):
    import numpy as np
    import concourse.bacc as bacc
    from concourse.bass_utils import run_bass_kernel_spmd

    nc = bacc.Bacc("TRN2", target_bir_lowering=False, num_devices=1)
    data = {**inputs, **shape_constants(np)}
    arrays, io = {}, {}
    for name in INS:
        a = np.ascontiguousarray(data[name])
        arrays[f"in_{name}"] = a
        io[name] = nc.dram_tensor(f"in_{name}", a.shape, mybir.dt.from_np(a.dtype), kind="ExternalInput").ap()
    for name, shape in OUTS:
        io[name] = nc.dram_tensor(f"out_{name}", shape, F32, kind="ExternalOutput").ap()
    build(nc, io)
    r = run_bass_kernel_spmd(nc, [arrays], core_ids=[0])
    return tuple(r.results[0][f"out_{name}"] for name, _ in OUTS)
```

```python
from contextlib import ExitStack

import concourse.bass as bass
from concourse import mybir

ALU = mybir.AluOpType
ACT = mybir.ActivationFunctionType
AX = mybir.AxisListType
F32 = mybir.dt.float32
F32R = mybir.dt.float32r

P = 128
D = 2048
KB = D // P
SEQ = 256
NB = 8
DS = 8
SAMP = NB * DS
T = SEQ + SAMP
NC_ = NB + 1
D_FF = 5504
FB = D_FF // P
CB = 8
CHUNKS = FB // CB
TAIL = FB - CHUNKS * CB
LRU = 1024
LH = LRU // P
CONV = 4
NH = 8
NKV = 2
GRP = NH // NKV
WIN = 128
N_MOD = 9
EPS = 1e-6
SCALE = float(P) ** -0.5
GELU_C = 0.7978845608028654
PAST = 2048

RAW = 8
SPLIT = 4
UNIT = 1024
HB = UNIT // P
ACC = 4
TU = 2 * TAIL * P

U_F1 = 2 * 4 * 8
G_F1 = KB
CH_U = CB * 4 + KB
CH_G = CB * 2 + KB
MOD_U = 4 * 8
TAIL_U = TAIL * 4 + KB // 2
TAIL_G = TAIL * 2 + KB
U_MIX = U_F1 + CHUNKS * CH_U + 7 * MOD_U + TAIL_U
G_MIX = G_F1 + CHUNKS * CH_G + TAIL_G
MIX_BLOCKS = 4 + NKV * (GRP + 2 * GRP)
U_OUT = U_MIX + 2 * MIX_BLOCKS
G_OUT = G_MIX + MIX_BLOCKS + 2 * LH
U_F2 = U_OUT + 2 * KB
G_F2 = G_OUT + KB
U_END = U_F2 + CHUNKS * CH_U + TAIL_U
ACT_FREED = 4 * LH

X_OUT = (CHUNKS + 1) * KB
X_F2 = X_OUT + KB
H_BASE = (0, KB, 3 * KB)
Q = KB // 4
IN_TURN = ((0, 0), (0, 1), (1, 0), (1, 1))
SIDE_BY_SIDE = ((0, 0), (1, 0), (0, 1), (1, 1))

X_AT = 12
RMS_AT = X_AT + KB + 4
MOD_AT = [*range(RMS_AT + 4, RMS_AT + 4 + 2 * Q), *range(48, 48 + Q)]
SET_UP = 2


def mixer_plan():
    order = [(24 + kv, "k", kv, 0) for kv in range(NKV)] + [(26 + kv, "v", kv, 0) for kv in range(NKV)]
    for kv in range(NKV):
        order += [(16 + GRP * kv + h, "q", kv, h) for h in range(GRP)]
        for h in range(GRP):
            order += [(GRP * kv + h, "x", kv, h), (LH + GRP * kv + h, "y", kv, h)]
    groups, freed, by = [], [], {"V": G_MIX, "A": 0}
    for _, kind, _, _ in order:
        groups.append(G_MIX + len(freed))
        for _ in range(3 if kind == "y" else 1):
            who = "A" if kind in "xy" else "V"
            by[who] += 1
            freed.append((who, by[who]))
    return [o[0] for o in order], [o[1:] for o in order], groups, freed


MIX_ORDER, MIX_KIND, MIX_GROUP, MIX_FREED = mixer_plan()
PRM_DMAS = 14
TOK_DMAS = 2 + 2 * NB

C_NORM, C_CW, C_CB, C_BA, C_BX, C_LAM, C_ADAB = 0, 64, 96, 104, 112, 120, 128
C_SCONV = C_ADAB + N_MOD * KB
C_SLRU = C_SCONV + NB * 3 * LH
N_PRM = C_SLRU + NB * LH

INS = ['x_prompt', 'x_sample', 'c_prompt', 'c_sample', 'state_conv', 'state_lru', 'cache_k_win', 'cache_v_win',
       'ada_w', 'ada_b', 'norm_ffn1', 'norm_mix', 'norm_ffn2', 'ffn1_w_gate', 'ffn1_w_up', 'ffn1_w_down',
       'w_in', 'conv_w', 'conv_b', 'lru_w_a', 'lru_b_a', 'lru_w_x', 'lru_b_x', 'lru_lambda', 'attn_sinks',
       'w_out', 'ffn2_w_gate', 'ffn2_w_up', 'ffn2_w_down', 'norm_final', 'identity', 'tables']
OUTS = [('y_prompt', (1, SEQ, D)), ('y_sample', (NB, DS, D)),
        ('conv_prompt', (1, 1, 3, LRU)), ('lru_prompt', (1, 1, LRU)),
        ('k_prompt', (1, 1, WIN, NKV, P)), ('v_prompt', (1, 1, WIN, NKV, P)),
        ('conv_sample', (1, NB, 3, LRU)), ('lru_sample', (1, NB, LRU)),
        ('k_sample', (1, NB, WIN, NKV, P)), ('v_sample', (1, NB, WIN, NKV, P))]


def build(nc, io):
    ctx = ExitStack()
    with ctx:
        def sb(name, shape, dt=F32):
            return ctx.enter_context(nc.sbuf_tensor(name, shape, dt))

        def sem(name):
            return ctx.enter_context(nc.semaphore(name))

        raw = sb("raw", [P, RAW, UNIT])
        hi = sb("hi", [P, SPLIT, UNIT], F32R)
        lo = sb("lo", [P, SPLIT, UNIT], F32R)
        x = sb("x", [P, KB, T])
        h_hi = sb("h_hi", [P, KB, T], F32R)
        h_lo = sb("h_lo", [P, KB, T], F32R)
        mod = sb("mod", [P, N_MOD * KB, NC_])
        prm = sb("prm", [P, N_PRM])
        ident = sb("ident", [P, P])
        ones = sb("ones", [P, P])[:, :]
        c_t = sb("c_t", [P, KB, 32])
        small = sb("small", [P, 96])
        with nc.sbuf_tensor("a_hi", [P, CB, T], F32R) as a_hi, nc.sbuf_tensor("a_lo", [P, CB, T], F32R) as a_lo:
            pass
        work = sb("work", [P, 18750])

        def carve(at, *shape):
            n = 1
            for s in shape:
                n *= s
            v = work[:, at:at + n]
            if len(shape) == 2:
                v = v.rearrange("p (a b) -> p a b", b=shape[1])
            if len(shape) == 3:
                v = v.rearrange("p (a b c) -> p a b c", b=shape[1], c=shape[2])
            return v, at + n

        at = 2 * CB * T
        silu_g, at = carve(at, 2, T)
        prod, at = carve(at, 2, T)
        xn, at = carve(at, 3, T)
        h_samp, at = carve(at, KB, SAMP)
        mod_row, at = carve(at, 256)
        rstd, at = carve(at, T)
        ln_ms, at = carve(at, T)
        sum_sq, at = carve(at, T)
        sq, ffn_end = carve(at, 2, T)
        x_tok, _ = carve(0, 3, D)
        c_tok, _ = carve(3 * D, D)
        prm_tok, at2 = carve(11072, 5, P)
        y_tok, _ = carve(0, 3, D)
        mix, at = carve(0, KB, T)
        k_t, at = carve(at, NKV, T)
        swapped, at = carve(at, T)
        ck_t, at = carve(at, NB, P)
        q_p, at = carve(at, GRP, SEQ)
        q_s, at = carve(at, NB, GRP, DS)
        tok, at = carve(at, 5, NKV, P)
        score, at = carve(at, 3 * P)
        probs_t, at = carve(at, 3 * P)
        rope_c, rope_s = score[:, 0:T], probs_t[:, 0:T]
        v_t, _ = carve(at, NKV, T)
        xb_p, at = carve(at, 3 + SEQ)
        xb_s, at = carve(at, NB, 3 + DS)
        xc2, at = carve(at, 2, T)
        yf, at = carve(at, T)
        gel, at = carve(at, T)
        th_r, at = carve(at, T)
        th_x, at = carve(at, T)
        root = th_r
        a_p, at = carve(at, SEQ)
        a_s, at = carve(at, NB, 1 + DS)
        u_p, at = carve(at, SEQ)
        u_s, at = carve(at, NB, 1 + DS)
        hs_p, at = carve(at, SEQ)
        hs_s, at = carve(at, NB, 1 + DS)
        st, at = carve(at, 288)
        early = at
        tables, at = carve(at, 2 * 3 * P + 4 + 2 * T)
        ck_tok, at = carve(at, NB, P)
        cv_tok, at = carve(at, NB, P)
        w_a, at = carve(at, GRP, P)
        w_x, at = carve(at, GRP, P)
        assert at <= 18750 and early >= ffn_end, (at, early)
        mask_p = tables[:, 0:3 * P]
        mask_s = [tables[:, 3 * P + (P + SAMP) * b:3 * P + (P + SAMP) * (b + 1)] for b in range(2)]
        group_of = tables[:, 6 * P:6 * P + 4]
        cos = tables[:, 6 * P + 4:6 * P + 4 + T]
        sin = tables[:, 6 * P + 4 + T:6 * P + 4 + 2 * T]
        sinks = small[:, 0:8]
        sink_s = small[:, 8:10]
        m2sp = small[:, 10:18]
        m4sp = small[:, 18:26]
        half_ba = small[:, 26:34]
        half_bx = small[:, 34:42]
        top = small[:, 42:44]
        neg_top = small[:, 44:46]
        den = small[:, 46:48]
        sink_e = small[:, 48:50]
        sp_e = small[:, 50:58]
        sp_q = small[:, 58:66]
        sp_s = small[:, 66:74]
        sink_pick = small[:, 74:78]
        eps = small[:, 78:79]
        warm = small[:, 79:80]
        final_norm = small[:, 80:96]

        psum = ctx.enter_context(nc.psum_tensor("ps", [P, 8, 512], F32))
        acc = [psum[:, b, 0:T] for b in range(ACC)]
        B_MOD, B_MODT, B_NORM = 4, 6, 7
        B_SCORE, B_PT, B_TOK, B_O = 4, 5, 6, 7

        landed = [sem(f"landed{i}") for i in range(RAW)]
        hi_done = sem("hi_done")
        lo_done = sem("lo_done")
        unit_done = sem("unit_done")
        dve_freed = sem("dve_freed")
        act_freed = sem("act_freed")
        c_in, prm_in, ident_in, x_in, tables_in = map(sem, ("c_in", "prm_in", "ident_in", "x_in", "tables_in"))
        ck_in, cv_in, gates_in, sinks_in = map(sem, ("ck_in", "cv_in", "gates_in", "sinks_in"))
        set_up = sem("set_up")
        c_silu, c_turned, prm_turned, c_ready, prm_ready = map(sem, ("c_silu", "c_turned", "prm_turned", "c_ready", "prm_ready"))
        x_turned = sem("x_turned")
        mod_row_ready = sem("mod_row_ready")
        mod_turned = sem("mod_turned")
        mod_half = sem("mod_half")
        mod_done = sem("mod_done")
        x_done = sem("x_done")
        squared = sem("squared")
        summed = sem("summed")
        ms_ready, rstd_ready = sem("ms_ready"), sem("rstd_ready")
        scale_ready = sem("scale_ready")
        xn_ready, h_hi_ready, h_ready = map(sem, ("xn_ready", "h_hi_ready", "h_ready"))
        samp_ready, samp_hi_ready, samp_lo_ready = map(sem, ("samp_ready", "samp_hi_ready", "samp_lo_ready"))
        silu_ready, a_hi_ready, a_ready = map(sem, ("silu_ready", "a_hi_ready", "a_ready"))
        swapped_ready, rope_done, tok_turned, tok_ready, tok_stored = map(
            sem, ("swapped_ready", "rope_done", "tok_turned", "tok_ready", "tok_stored"))
        ck_turned, ck_ready = sem("ck_turned"), sem("ck_ready")
        scored, masked, maxed, exp_done, probs_ready, pt_turned, pt_copied, o_ready, o_copied = map(
            sem, ("scored", "masked", "maxed", "exp_done", "probs_ready", "pt_turned", "pt_copied", "o_ready", "o_copied"))
        xc_ready, gates_ready, gate_acts, gel_z, gel_t, lru_done, state_saved = map(
            sem, ("xc_ready", "gates_ready", "gate_acts", "gel_z", "gel_t", "lru_done", "state_saved"))
        gelu_ready = sem("gelu_ready")
        xb_state = sem("xb_state")
        xn_y, y_turned, y_copied = sem("xn_y"), sem("y_turned"), sem("y_copied")
        st_turned, st_copied = sem("st_turned"), sem("st_copied")
        sp_ready, sp_exp = sem("sp_ready"), sem("sp_exp")
        act_chain, dve_chain, pool_chain = sem("act_chain"), sem("dve_chain"), sem("pool_chain")
        stored = sem("stored")
        cache_stored, state_stored = sem("cache_stored"), sem("state_stored")

        def plus(n, turns, per):
            return n if turns is None else turns * per + n

        def raw_slot(u):
            return raw[:, u % RAW, :]

        def hi_slot(u):
            return hi[:, u % SPLIT, :]

        def lo_slot(u):
            return lo[:, u % SPLIT, :]

        def bank(g):
            return acc[g % ACC]

        def sample(v):
            return v[:, SEQ:T].rearrange("p (b s) -> p b s", s=DS)

        def unit_floats(u):
            for end in (U_MIX, U_END):
                if end - KB // 2 <= u < end:
                    return TU
            return UNIT

        block = ctx.enter_context(nc.Block())

        @block.sync
        def _(sp):
            def load(u, turns, src, shape=(HB, P)):
                if u >= RAW or turns is not None:
                    sp.wait_ge(unit_done, plus(u - RAW + 1, turns, RAW))
                dst = raw_slot(u)[:, 0:shape[0] * shape[1]].rearrange("p (k n) -> p k n", n=shape[1])
                sp.dma_start(dst, src).then_inc(landed[u % RAW], 16)

            def blocks(w):
                return w.rearrange("(k p) n -> p k n", p=P)

            ada = blocks(io['ada_w'][0])

            def mod_unit(u, turns, group, part):
                load(u, turns, ada[:, 2 * part:2 * part + 2, bass.ds(group * 512, 512)], (2, 512))

            def columns(u, turns, w, half, col):
                load(u, turns, w[:, half * HB:(half + 1) * HB, bass.ds(col, P)])

            for part in range(16):
                mod_unit(part, None, part // 8 * Q, part % 8)
            with sp.Fori(0, 3) as i:
                for part in range(16):
                    mod_unit(16 + part, i * 2, i + (1 + part // 8 * Q), part % 8)

            def ffn(u0, gate, up, down, with_mod):
                gate, up, down = blocks(gate), blocks(up), blocks(down)

                def up_pair(u, turns, col, group):
                    for n in range(8):
                        w, half = (SIDE_BY_SIDE if group is None else IN_TURN)[n % 4]
                        if group is not None:
                            mod_unit(u, turns, group, n)
                            u += 1
                        columns(u, turns, (gate, up)[w], half, col + P * (n // 4))
                        u += 1

                def down_eight(u, turns, row, col, group):
                    for n in range(8):
                        if group is not None:
                            mod_unit(u, turns, group, n)
                            u += 1
                        load(u, turns, down[:, bass.ds(row, CB), bass.ds(col + P * n, P)])
                        u += 1

                def chunk(u, chunk_turns, c, group, mod_up, mod_down):
                    per = 2 if mod_up else 1
                    with sp.Fori(0, 4) as i:
                        up_pair(u, chunk_turns + i * per, c * (CB * P) + i * (2 * P), group + i if mod_up else None)
                    u += CB * 4 * per
                    per = 2 if mod_down else 1
                    with sp.Fori(0, 2) as i:
                        down_eight(u, chunk_turns + i * per, c * CB, i * (CB * P),
                                   group + 4 + i if mod_down else None)
                    return u + KB * per

                if with_mod:
                    with sp.Fori(0, 4) as c:
                        chunk(u0, c * 12, c, c * 6 + 8, True, True)
                    u = chunk(u0 + 4 * 96, 0, 4, 32, True, False)
                else:
                    with sp.Fori(0, CHUNKS) as c:
                        chunk(u0, c * 6, c, 0, False, False)
                    u = u0 + CHUNKS * CH_U
                for s in range(TAIL):
                    for n in range(4):
                        columns(u, None, (gate, up)[n // 2], n % 2, (CHUNKS * CB + s) * P)
                        u += 1
                for n in range(KB // 2):
                    load(u, None, down[:, CHUNKS * CB:FB, n * 2 * P:(n + 1) * 2 * P], (TAIL, 2 * P))
                    u += 1

            ffn(U_F1, io['ffn1_w_gate'][0], io['ffn1_w_up'][0], io['ffn1_w_down'][0], True)

            w_in = blocks(io['w_in'][0])
            for n, (w, half) in enumerate(SIDE_BY_SIDE):
                columns(U_MIX + n, None, w_in, half, MIX_ORDER[w] * P)
            for n, col in list(enumerate(MIX_ORDER))[2:]:
                for half in range(2):
                    columns(U_MIX + 2 * n + half, None, w_in, half, col * P)
                if n == 12:
                    sp.wait_ge(tok_ready, NKV)
                    sp.dma_start(io['v_prompt'][0, 0], tok[:, 1]).then_inc(tok_stored, 16)
                    sp.dma_start(io['k_prompt'][0, 0], tok[:, 3]).then_inc(tok_stored, 16)
                    for b in range(NB):
                        rows = slice(b * DS, (b + 1) * DS)
                        sp.dma_start(io['v_sample'][0, b, WIN - DS:], tok[rows, 2]).then_inc(tok_stored, 16)
                        sp.dma_start(io['k_sample'][0, b, WIN - DS:], tok[rows, 4]).then_inc(tok_stored, 16)

            w_out = blocks(io['w_out'][0])
            for i in range(4):
                for half in range(2):
                    for m in range(4):
                        columns(U_OUT + 8 * i + 4 * half + m, None, w_out, 1 - half, (4 * i + m) * P)

            ffn(U_F2, io['ffn2_w_gate'][0], io['ffn2_w_up'][0], io['ffn2_w_down'][0], False)

            ys = io['y_sample'].rearrange("b s n -> (b s) n")
            for q in range(4):
                sp.wait_ge(y_copied, 4 * (q + 1))
                cols = slice(4 * q * P, 4 * (q + 1) * P)
                for t in range(2):
                    sp.dma_start(io['y_prompt'][0, t * P:(t + 1) * P, cols], y_tok[:, t, cols]).then_inc(stored, 16)
                sp.dma_start(ys[:, cols], y_tok[0:SAMP, 2, cols]).then_inc(stored, 16)
            sp.wait_ge(stored, 12 * 16)
            sp.wait_ge(tok_stored, TOK_DMAS * 16)
            sp.wait_ge(cache_stored, 2 * 16)
            sp.wait_ge(state_stored, 5 * 16)

        @block.tensor
        def _(pe):
            mm = nc.tensor.matmul

            def turn(out, in_, n):
                return nc.tensor.transpose(out, in_, ident[0:n, 0:n])

            def arrive(u, turns):
                pe.wait_ge(lo_done, plus(u + 1, turns, RAW))

            def free_bank(g, gturns, freed_before=0):
                if g - ACC - freed_before >= 0 or gturns is not None:
                    pe.wait_ge(dve_freed, plus(g - ACC + 1 - freed_before, gturns, ACC))

            def products(out, u, j, cols, col, r_hi, r_lo, first, last):
                w_hi = hi_slot(u)[:, j * cols + col:j * cols + col + P]
                w_lo = lo_slot(u)[:, j * cols + col:j * cols + col + P]
                mm(out, w_hi, r_hi, start=first, stop=False)
                mm(out, w_hi, r_lo, start=False, stop=False)
                return mm(out, w_lo, r_hi, start=False, stop=last)

            def mod_unit(u, turns, part, group):
                arrive(u, turns)
                if part == 0 and group is not None:
                    pe.wait_ge(mod_row_ready, group)
                for j in range(2):
                    for h in range(2):
                        rows = slice(32 * (2 * j + h), 32 * (2 * j + h + 1))
                        last = mm(psum[rows, B_MOD, 0:256], c_t[:, 2 * part + j, :],
                                  raw_slot(u)[:, j * 512 + h * 256:j * 512 + (h + 1) * 256], start=(part == 0), stop=(part == 7))
                last.then_inc(unit_done, 1)

            def mod_turn(group):
                pe.wait_ge(mod_row_ready, group + 1)
                if not isinstance(group, int) or group > 0:
                    pe.wait_ge(mod_done, group)
                for j in range(2):
                    last = turn(psum[:, B_MODT, j * P:(j + 1) * P], mod_row[:, j * P:(j + 1) * P], P)
                last.then_inc(mod_turned, 1)

            pe.wait_ge(ident_in, 16)
            pe.wait_ge(c_silu, 1)
            for k in range(KB):
                last = turn(psum[:, 5, NC_ * k:NC_ * (k + 1)], c_tok[0:NC_, k * P:(k + 1) * P], NC_)
            last.then_inc(c_turned, 1)
            def turn_parameters():
                pe.wait_ge(prm_in, PRM_DMAS * 16)
                for k in range(4):
                    turn(psum[:, B_NORM, P * k:P * (k + 1)], prm_tok[:, k, :], P)
                turn(psum[:, B_MODT, 0:16], prm_tok[0:16, 4, :], 16).then_inc(prm_turned, 1)

            def turn_x(k):
                if k >= ACC:
                    pe.wait_ge(dve_freed, k - ACC + 1)
                for t in range(2):
                    turn(bank(k)[:, t * P:(t + 1) * P], x_tok[:, t, k * P:(k + 1) * P], P)
                turn(bank(k)[:, SEQ:T], x_tok[0:SAMP, 2, k * P:(k + 1) * P], SAMP).then_inc(x_turned, 1)

            def sum_of_squares(n):
                pe.wait_ge(summed, n * KB + KB)
                mm(psum[:, B_NORM, 0:T], ones, sum_sq, start=True, stop=True).then_inc(ms_ready, 1)

            pe.wait_ge(c_ready, 1)
            for g in range(8):
                for part in range(8):
                    mod_unit(8 * g + part, None, part, g if g else None)
                    k = 8 * g + part - X_AT
                    if k == 0:
                        pe.wait_ge(x_in, 3 * 16)
                    if 0 <= k < KB:
                        turn_x(k)
                    if 8 * g + part == RMS_AT:
                        sum_of_squares(0)
                if g == 0:
                    turn_parameters()
                    pe.wait_ge(prm_ready, 1)
                mod_turn(g)

            def project(u, turns, g, gturns, h0, freed_before=0):
                out = bank(g)
                for half in range(2):
                    arrive(u + half, turns)
                    if half == 0 and freed_before is not None:
                        free_bank(g, gturns, freed_before)
                    for j in range(HB):
                        k = half * HB + j
                        pe.wait_ge(h_ready, h0 + k + 1)
                        last = products(out, u + half, j, P, 0, h_hi[:, k, :], h_lo[:, k, :], k == 0, k == KB - 1)
                    last.then_inc(unit_done, 1)

            def side_by_side(u, turns, out, h0):
                for half in range(2):
                    for w in range(2):
                        arrive(u + 2 * half + w, turns)
                    for j in range(HB):
                        k = half * HB + j
                        pe.wait_ge(h_ready, h0 + k + 1)
                        for w in range(2):
                            last = products(out[w], u + 2 * half + w, j, P, 0, h_hi[:, k, :], h_lo[:, k, :], k == 0, k == KB - 1)
                            if j == HB - 1:
                                last.then_inc(unit_done, 1)

            def ffn(u0, g0, h0, a0, freed_before, with_mod):
                def up_pair(u, turns, g, gturns, group):
                    for step in range(2):
                        if group is not None:
                            for n, (w, half) in enumerate(IN_TURN):
                                mod_unit(u, turns, 4 * step + n, group)
                                arrive(u + 1, turns)
                                if half == 0:
                                    free_bank(g + w, gturns, freed_before)
                                for j in range(HB):
                                    k = half * HB + j
                                    pe.wait_ge(h_ready, h0 + k + 1)
                                    last = products(bank(g + w), u + 1, j, P, 0, h_hi[:, k, :], h_lo[:, k, :], k == 0, k == KB - 1)
                                last.then_inc(unit_done, 1)
                                u += 2
                        else:
                            for w in range(2):
                                free_bank(g + w, gturns, freed_before)
                            side_by_side(u, turns, (bank(g), bank(g + 1)), h0)
                            u += 4
                        g += 2
                    if group is not None:
                        mod_turn(group)

                def down_eight(u, turns, g, gturns, a_before, group):
                    for n in range(8):
                        if group is not None:
                            mod_unit(u, turns, n, group)
                            u += 1
                        arrive(u, turns)
                        free_bank(g, gturns, freed_before)
                        for j in range(CB):
                            pe.wait_ge(a_ready, a_before + (j + 1))
                            last = products(bank(g), u, j, P, 0, a_hi[:, j, :], a_lo[:, j, :], j == 0, j == CB - 1)
                        last.then_inc(unit_done, 1)
                        u += 1
                        g += 1
                    if group is not None:
                        mod_turn(group)

                def chunk(u, turns, g, gturns, a_before, group, mod_up, mod_down):
                    per = 2 if mod_up else 1
                    with pe.Fori(0, 4) as i:
                        up_pair(u, turns + i * per, g, gturns + i, group + i if mod_up else None)
                    u, g = u + CB * 4 * per, g + 2 * CB
                    per = 2 if mod_down else 1
                    with pe.Fori(0, 2) as i:
                        down_eight(u, turns + i * per, g, gturns + i * 2, a_before,
                                   group + 4 + i if mod_down else None)
                    return u + KB * per, g + KB

                if with_mod:
                    with pe.Fori(0, 4) as c:
                        chunk(u0, c * 12, g0, c * 8, c * CB + a0, c * 6 + 8, True, True)
                    u, g = chunk(u0 + 4 * 96, 0, g0 + 4 * CH_G, 0, a0 + 4 * CB, 32, True, False)
                else:
                    with pe.Fori(0, CHUNKS) as c:
                        chunk(u0, c * 6, g0, c * 8, c * CB + a0, 0, False, False)
                    u, g = u0 + CHUNKS * CH_U, g0 + CHUNKS * CH_G
                for s in range(2 * TAIL):
                    project(u, None, g, None, h0, freed_before)
                    u, g = u + 2, g + 1
                for n in range(KB // 2):
                    arrive(u, None)
                    for m in range(2):
                        free_bank(g, None, freed_before)
                        for j in range(TAIL):
                            pe.wait_ge(a_ready, a0 + CHUNKS * CB + j + 1)
                            last = products(bank(g), u, j, 2 * P, m * P, a_hi[:, j, :], a_lo[:, j, :], j == 0,
                                            j == TAIL - 1)
                        g += 1
                    last.then_inc(unit_done, 1)
                    u += 1

            ffn(U_F1, G_F1, 0, 0, 0, True)
            sum_of_squares(1)

            def mix_free_bank(n):
                g = MIX_GROUP[n]
                freed_sem, count = MIX_FREED[g - ACC - G_MIX] if g - ACC >= G_MIX else ("V", g - ACC + 1)
                pe.wait_ge(dve_freed if freed_sem == "V" else act_freed, count)
                return g

            def mix_project(n):
                g = mix_free_bank(n)
                project(U_MIX + 2 * n, None, g, None, KB, None)

            def token_major(kv):
                pe.wait_ge(rope_done, kv + 1)
                pe.wait_ge(dve_freed, MIX_FREED[2 + kv][1])
                if kv:
                    pe.wait_ge(tok_ready, kv)
                turn(psum[:, B_TOK, 0:P], v_t[:, kv, 0:P], P)
                turn(psum[:, B_TOK, P:2 * P], v_t[:, kv, P:2 * P], P)
                turn(psum[:, B_TOK, 2 * P:3 * P], k_t[:, kv, P:2 * P], P)
                turn(psum[0:SAMP, B_TOK, 3 * P:4 * P], v_t[:, kv, SEQ:T], P)
                turn(psum[0:SAMP, B_O, 0:P], k_t[:, kv, SEQ:T], P).then_inc(tok_turned, 1)

            def cached_keys(kv, half):
                pe.wait_ge(ck_in, 16 * (kv + 1))
                n = 2 * kv + half
                if n:
                    pe.wait_ge(ck_ready, n)
                if half == 0 and kv:
                    pe.wait_ge(pt_copied, 6 * kv)
                for b in range(4):
                    last = turn(psum[:, B_PT, b * P:(b + 1) * P], ck_tok[:, 4 * half + b, :], P)
                last.then_inc(ck_turned, 1)

            def scores(kv, t):
                job = 6 * kv + t
                if t == 0:
                    pe.wait_ge(rope_done, NKV + GRP * (kv + 1))
                    pe.wait_ge(ck_ready, 2 * (kv + 1))
                if job:
                    pe.wait_ge(masked, job)
                out = psum[:, B_SCORE, :]
                if t < GRP:
                    mm(out[:, 0:P], q_p[:, t, 0:P], k_t[:, kv, 0:P], start=True, stop=True)
                    last = mm(out[:, P:3 * P], q_p[:, t, P:SEQ], k_t[:, kv, 0:SEQ], start=True, stop=True)
                else:
                    b0 = 4 * (t - GRP)
                    for b in range(4):
                        mm(out[32 * b:32 * b + 32, 0:P], q_s[:, b0 + b, :, :].rearrange("p g s -> p (g s)"),
                           ck_t[:, b0 + b, :], start=True, stop=True)
                    last = mm(out[:, P:P + SAMP], q_s[:, b0:b0 + 4, :, :].rearrange("p b g s -> p (b g s)"),
                              k_t[:, kv, SEQ:T], start=True, stop=True)
                last.then_inc(scored, 1)

            def turn_probs(kv, t):
                job = 6 * kv + t
                pe.wait_ge(probs_ready, job + 1)
                if job:
                    pe.wait_ge(pt_copied, job)
                if t == 0:
                    pe.wait_ge(ck_ready, 2 * (kv + 1))
                out = psum[:, B_PT, :]
                if t < GRP:
                    for j in range(3):
                        last = turn(out[:, j * P:(j + 1) * P], score[:, j * P:(j + 1) * P], P)
                else:
                    turn(out[:, 0:P], score[:, 0:P], P)
                    last = turn(out[0:SAMP, P:2 * P], score[:, P:P + SAMP], P)
                last.then_inc(pt_turned, 1)

            def values(kv, t):
                job = 6 * kv + t
                pe.wait_ge(pt_copied, job + 1)
                if job:
                    pe.wait_ge(o_copied, job)
                if t == 0:
                    pe.wait_ge(tok_ready, NKV)
                out = psum[:, B_O, :]
                if t < GRP:
                    mm(out[:, 0:P], tok[:, 0, kv, :], probs_t[:, 0:P], start=True, stop=True)
                    mm(out[:, P:2 * P], tok[:, 0, kv, :], probs_t[:, P:2 * P], start=True, stop=False)
                    last = mm(out[:, P:2 * P], tok[:, 1, kv, :], probs_t[:, 2 * P:3 * P], start=False, stop=True)
                else:
                    if t == GRP:
                        pe.wait_ge(cv_in, 16 * (kv + 1))
                    mm(out[:, 0:P], tok[0:SAMP, 2, kv, :], probs_t[0:SAMP, P:2 * P], start=True, stop=False)
                    for b in range(4):
                        last = mm(out[:, 32 * b:32 * b + 32], cv_tok[:, 4 * (t - GRP) + b, :],
                                  probs_t[:, 32 * b:32 * b + 32], start=False, stop=(b == 3))
                last.then_inc(o_ready, 1)

            def attend(kv, t):
                if t >= 2:
                    values(kv, t - 2)
                if 1 <= t <= 6:
                    turn_probs(kv, t - 1)
                if t < 6:
                    scores(kv, t)

            def gates(kv, h, n):
                head = GRP * kv + h
                pe.wait_ge(xc_ready, head + 1)
                if h == 0:
                    pe.wait_ge(gates_in, 32 * (kv + 1))
                for k, w in enumerate((w_a, w_x)):
                    g = MIX_GROUP[n] + 1 + k
                    freed_sem, count = MIX_FREED[g - ACC - G_MIX]
                    pe.wait_ge(dve_freed if freed_sem == "V" else act_freed, count)
                    last = mm(bank(g), w[:, h, :], xc2[:, head % 2, :], start=True, stop=True)
                last.then_inc(gates_ready, 1)

            side_by_side(U_MIX, None, [bank(mix_free_bank(n)) for n in range(2)], KB)
            for n in range(2, 4):
                mix_project(n)
            n = 4
            for kv in range(NKV):
                for q in range(GRP):
                    mix_project(n)
                    n += 1
                    if q < 2:
                        if kv == 0:
                            token_major(q)
                        cached_keys(kv, q)
                for h in range(GRP):
                    mix_project(n)
                    n += 1
                    attend(kv, 2 * h)
                    mix_project(n)
                    gates(kv, h, n)
                    n += 1
                    attend(kv, 2 * h + 1)

            with pe.Fori(0, 4) as i:
                for half in range(2):
                    for m in range(4):
                        u = U_OUT + 4 * half + m
                        arrive(u, i)
                        if half == 0:
                            pe.wait_ge(act_freed, ACT_FREED - ACC + m + 1)
                            free_bank(G_OUT + m, i, ACT_FREED)
                        for j in range(HB):
                            n = half * HB + j
                            k = (LH + n) % KB
                            pe.wait_ge(h_ready, 2 * KB + n + 1)
                            last = products(bank(G_OUT + m), u, j, P, 0, h_hi[:, k, :], h_lo[:, k, :], n == 0, n == KB - 1)
                        last.then_inc(unit_done, 1)

            pe.wait_ge(state_saved, LH)
            for t in range(2):
                turn(psum[:, B_SCORE, t * P:(t + 1) * P], st[:, t * P:(t + 1) * P], P)
            turn(psum[0:32, B_SCORE, 2 * P:3 * P], st[:, 2 * P:2 * P + 32], P).then_inc(st_turned, 1)

            sum_of_squares(2)
            ffn(U_F2, G_F2, 3 * KB, FB, ACT_FREED, False)
            sum_of_squares(3)

            for k in range(KB):
                pe.wait_ge(xn_y, k + 1)
                if k >= 2:
                    pe.wait_ge(y_copied, k - 1)
                out = psum[:, 4 + k % 2, :]
                for t in range(2):
                    turn(out[:, t * P:(t + 1) * P], xn[:, k % 3, t * P:(t + 1) * P], P)
                turn(out[0:SAMP, 2 * P:3 * P], xn[:, k % 3, SEQ:T], P).then_inc(y_turned, 1)

        @block.scalar
        def _(act):
            run = nc.scalar.activation
            chained = [0]

            def chain(instruction):
                chained[0] += 1
                instruction.then_inc(act_chain, 1)
                act.wait_ge(act_chain, chained[0])

            def split(u, turns=None, mod_unit=False):
                n = 1 if mod_unit else unit_floats(u)
                act.wait_ge(landed[u % RAW], plus(16 * (u // RAW + 1), turns, 16))
                run(hi_slot(u)[:, 0:n], raw_slot(u)[:, 0:n], ACT.Copy).then_inc(hi_done, 1)

            def finished(u, turns=None):
                act.wait_ge(unit_done, plus(u + 1, turns, RAW))

            def copy_mod():
                run(mod_row, psum[:, B_MOD, 0:256], ACT.Copy).then_inc(mod_row_ready, 1)

            act.dma_start(c_tok[0:1, :], io['c_prompt']).then_inc(c_in, 16)
            act.dma_start(c_tok[1:NC_, :], io['c_sample']).then_inc(c_in, 16)
            act.dma_start(ident[:, :], io['identity']).then_inc(ident_in, 16)
            for t in range(2):
                act.dma_start(x_tok[:, t, :], io['x_prompt'][0, t * P:(t + 1) * P, :]).then_inc(x_in, 16)
            act.dma_start(x_tok[0:SAMP, 2, :], io['x_sample'].rearrange("b s n -> (b s) n")).then_inc(x_in, 16)
            act.wait_ge(c_in, 32)
            run(c_tok[0:NC_, :], c_tok[0:NC_, :], ACT.Silu).then_inc(c_silu, 1)
            for u in range(SPLIT):
                split(u, None, True)

            def square(m, n, ready, count):
                act.wait_ge(ready, count)
                if n * KB + m >= 2:
                    act.wait_ge(summed, n * KB + m - 1)
                run(sq[:, m % 2, :], x[:, m, :], ACT.Square).then_inc(squared, 1)

            def rms(n):
                run(warm, eps, ACT.Ln)
                act.wait_ge(ms_ready, n + 1)
                chain(run(ln_ms, psum[:, B_NORM, 0:T], ACT.Ln, bias=eps, scale=1.0 / D))
                run(rstd, ln_ms, ACT.Exp, scale=-0.5).then_inc(rstd_ready, 1)

            def modulate(n, sh, first, end):
                for k in range(first, end):
                    if k % Q == 0:
                        act.wait_ge(samp_ready, n * 4 + k // Q + 1)
                        run(h_hi[:, k:k + Q, SEQ:T], h_samp[:, k:k + Q, :], ACT.Copy).then_inc(samp_hi_ready, 1)
                    act.wait_ge(xn_ready, n * KB + k + 1)
                    run(h_hi[:, k, 0:SEQ], xn[:, k % 3, 0:SEQ], ACT.Identity,
                        bias=mod[:, KB * sh + k, 0:1]).then_inc(h_hi_ready, 1)

            act.wait_ge(set_up, SET_UP)
            for u in range(U_F1):
                finished(u)
                if u % 8 == 7:
                    copy_mod()
                if X_AT < u <= X_AT + KB:
                    k = u - X_AT - 1
                    act.wait_ge(x_turned, k + 1)
                    run(x[:, k, :], bank(k), ACT.Copy).then_inc(dve_freed, 1)
                if X_AT + 1 < u <= X_AT + 1 + KB:
                    square(u - X_AT - 2, 0, dve_freed, u - X_AT - 1)
                if u - 1 in MOD_AT:
                    k = MOD_AT.index(u - 1)
                    modulate(0, 0, k, k + 1)
                split(u + SPLIT, None, u + SPLIT < U_F1 or u % 2 == 0)
                if u == 10:
                    act.wait_ge(sp_ready, 1)
                    run(sp_e, sp_e, ACT.Exp, scale=-1.0).then_inc(sp_exp, 1)
                if u == RMS_AT:
                    rms(0)
            modulate(0, 0, 3 * Q, KB)

            def ffn(u0, g0, x0, norm, with_mod):
                def silu(g, step):
                    run(silu_g[:, step % 2, :], bank(g), ACT.Silu).then_inc(silu_ready, 1)

                def up_pair(u, turns, g, with_group, last_mod):
                    for n in range(8):
                        w, half = (IN_TURN if with_group else SIDE_BY_SIDE)[n % 4]
                        if with_group:
                            finished(u, turns)
                            split(u + SPLIT, turns, not last_mod)
                            if n == 7:
                                copy_mod()
                            u += 1
                        finished(u, turns)
                        if w == 0 and half == 1:
                            silu(g + n // 4 * 2, n // 4)
                        split(u + SPLIT, turns)
                        u += 1

                def down_eight(u, turns, with_group):
                    for n in range(8):
                        if with_group:
                            finished(u, turns)
                            if n == 7:
                                copy_mod()
                            split(u + SPLIT, turns, True)
                            u += 1
                        finished(u, turns)
                        split(u + SPLIT, turns)
                        u += 1

                def chunk(u, turns, g, mod_up, mod_down):
                    per = 2 if mod_up else 1
                    with act.Fori(0, 4) as i:
                        up_pair(u, turns + i * per, g, mod_up, not mod_down)
                    u, g = u + CB * 4 * per, g + 2 * CB
                    per = 2 if mod_down else 1
                    with act.Fori(0, 2) as i:
                        down_eight(u, turns + i * per, mod_down)
                    return u + KB * per, g + KB

                if with_mod:
                    with act.Fori(0, 4) as c:
                        chunk(u0, c * 12, g0, True, True)
                    u, g = chunk(u0 + 4 * 96, 0, g0 + 4 * CH_G, True, False)
                else:
                    with act.Fori(0, CHUNKS) as c:
                        chunk(u0, c * 6, g0, False, False)
                    u, g = u0 + CHUNKS * CH_U, g0 + CHUNKS * CH_G
                for s in range(TAIL):
                    for n in range(4):
                        finished(u)
                        if n == 1:
                            silu(g, s)
                        split(u + SPLIT)
                        u += 1
                    g += 2
                for n in range(KB // 2):
                    finished(u)
                    if u + SPLIT < U_END:
                        split(u + SPLIT)
                    for m in range(2):
                        square(2 * n + m, norm, x_done, x0 + CHUNKS * KB + 2 * n + m + 1)
                    u += 1

            ffn(U_F1, G_F1, 0, 1, True)
            rms(1)
            modulate(1, 3, 0, KB)

            def evacuate(n):
                kind, kv, h = MIX_KIND[n]
                src = bank(MIX_GROUP[n])
                head = GRP * kv + h
                if kind in "kq":
                    r = kv if kind == "k" else NKV + head
                    if r:
                        act.wait_ge(rope_done, r)
                    run(swapped[0:64, :], src[64:128, :], ACT.Copy)
                    run(swapped[64:128, :], src[0:64, :], ACT.Copy).then_inc(swapped_ready, 1)
                if kind == "x":
                    if head:
                        act.wait_ge(xc_ready, head)
                    run(xb_p[:, 3:3 + SEQ], src[:, 0:SEQ], ACT.Copy)
                    run(xb_s[:, :, 3:3 + DS], sample(src), ACT.Copy).then_inc(act_freed, 1)
                if kind == "y":
                    if head:
                        act.wait_ge(lru_done, head)
                    run(yf, src, ACT.Copy)
                    run(gel, src, ACT.Square).then_inc(act_freed, 1)

            def gate_functions(kv, h, n):
                head = GRP * kv + h
                act.wait_ge(gates_ready, head + 1)
                if head:
                    act.wait_ge(lru_done, head)
                run(th_r, bank(MIX_GROUP[n] + 1), ACT.Tanh, scale=0.5, bias=half_ba[:, head:head + 1]).then_inc(act_freed, 1)
                run(th_x, bank(MIX_GROUP[n] + 2), ACT.Tanh, scale=0.5, bias=half_bx[:, head:head + 1]).then_inc(act_freed, 1)
                act.wait_ge(act_freed, 4 * head + 4)
                m4, m2 = m4sp[:, head:head + 1], m2sp[:, head:head + 1]
                run(a_p, th_r[:, 0:SEQ], ACT.Exp, scale=m4, bias=m4)
                chain(run(a_s[:, :, 1:1 + DS], sample(th_r), ACT.Exp, scale=m4, bias=m4))
                chain(run(root, th_r, ACT.Tanh, scale=m2, bias=m2))
                run(root, root, ACT.Sqrt, scale=-0.25).then_inc(gate_acts, 1)

            def gelu_tanh(head):
                act.wait_ge(gel_z, head + 1)
                run(gel, gel, ACT.Tanh, scale=GELU_C).then_inc(gel_t, 1)

            def copy_cached_keys(kv, half):
                act.wait_ge(ck_turned, 2 * kv + half + 1)
                run(ck_t[:, 4 * half:4 * half + 4, :], psum[:, B_PT, :].rearrange("p (b n) -> p b n", n=P),
                    ACT.Copy).then_inc(ck_ready, 1)

            def copy_probs(kv, t):
                act.wait_ge(pt_turned, 6 * kv + t + 1)
                if t < GRP:
                    run(probs_t, psum[:, B_PT, 0:3 * P], ACT.Copy).then_inc(pt_copied, 1)
                else:
                    run(probs_t[:, 0:P], psum[:, B_PT, 0:P], ACT.Copy)
                    run(probs_t[0:SAMP, P:2 * P], psum[0:SAMP, B_PT, P:2 * P], ACT.Copy).then_inc(pt_copied, 1)

            def copy_values(kv, t):
                act.wait_ge(o_ready, 6 * kv + t + 1)
                if t < GRP:
                    run(mix[:, LH + GRP * kv + t, 0:SEQ], psum[:, B_O, 0:SEQ], ACT.Copy).then_inc(o_copied, 1)
                else:
                    for g in range(GRP):
                        src = psum[:, B_O, 0:P].rearrange("p (b g s) -> p g b s", g=GRP, s=DS)[:, g]
                        dst = mix[:, LH + GRP * kv + g, SEQ + 32 * (t - GRP):SEQ + 32 * (t - GRP + 1)]
                        last = run(dst.rearrange("p (b s) -> p b s", s=DS), src, ACT.Copy)
                    last.then_inc(o_copied, 1)

            def exponents(kv, t):
                act.wait_ge(maxed, 6 * kv + t + 1)
                if t < GRP:
                    head = GRP * kv + t
                    run(score[:, 0:P], score[:, 0:P], ACT.Exp, bias=neg_top[:, 0:1], accum_out=den[:, 0:1])
                    run(score[:, P:3 * P], score[:, P:3 * P], ACT.Exp, bias=neg_top[:, 1:2], accum_out=den[:, 1:2])
                    run(sink_e[:, 0:2], neg_top[:, 0:2], ACT.Exp, bias=sinks[:, head:head + 1]).then_inc(exp_done, 1)
                else:
                    run(score[:, 0:P + SAMP], score[:, 0:P + SAMP], ACT.Exp, bias=neg_top[:, 0:1], accum_out=den[:, 0:1])
                    run(sink_e[:, 0:1], neg_top[:, 0:1], ACT.Exp, bias=sink_s[:, kv:kv + 1]).then_inc(exp_done, 1)

            def attended(kv, t):
                if t >= 2:
                    copy_values(kv, t - 2)
                if 1 <= t <= 6:
                    copy_probs(kv, t - 1)
                if t < 6:
                    exponents(kv, t)

            def operand(first, end):
                for k in range(first, end):
                    if k < LH:
                        act.wait_ge(lru_done, k + 1)
                    run(h_hi[:, k, :], mix[:, k, :], ACT.Copy).then_inc(h_hi_ready, 1)

            def behind(n):
                kind, kv, h = MIX_KIND[n]
                if kind == "q" and h < 2:
                    copy_cached_keys(kv, h)
                if kind == "x":
                    attended(kv, 2 * h)
                if kind == "y":
                    attended(kv, 2 * h + 1)
                    if n == MIX_BLOCKS - 1:
                        act.wait_ge(o_copied, 12)
                        operand(LH, KB)
                    gelu_tanh(GRP * kv + h)

            for n in range(MIX_BLOCKS):
                finished(U_MIX + 2 * n)
                if n == 1:
                    evacuate(0)
                split(U_MIX + 2 * n + SPLIT)
                finished(U_MIX + 2 * n + 1)
                if n:
                    evacuate(n)
                behind(n)
                split(U_MIX + 2 * n + 1 + SPLIT)
                if MIX_KIND[n][0] == "y" and n < MIX_BLOCKS - 1:
                    gate_functions(*MIX_KIND[n][1:], n)

            gate_functions(NKV - 1, GRP - 1, MIX_BLOCKS - 1)
            operand(0, LH)

            act.wait_ge(tok_stored, TOK_DMAS * 16)
            with act.Fori(0, 4) as i:
                for n in range(8):
                    finished(U_OUT + n, i)
                    split(U_OUT + n + SPLIT, i)
                    if n >= 4:
                        m = n - 4
                        act.wait_ge(x_done, i * 4 + X_OUT + m + 1)
                        act.wait_ge(summed, i * 4 + 2 * KB + m - 1)
                        run(sq[:, m % 2, :], x[:, bass.ds(i * 4 + m, 1), :].rearrange("p a n -> p (a n)"),
                            ACT.Square).then_inc(squared, 1)

            rms(2)
            modulate(2, 6, 0, KB)
            act.wait_ge(st_turned, 1)
            run(prm[:, 0:2 * P], psum[:, B_SCORE, 0:2 * P], ACT.Copy)
            run(prm[0:32, 2 * P:3 * P], psum[0:32, B_SCORE, 2 * P:3 * P], ACT.Copy).then_inc(st_copied, 1)
            ffn(U_F2, G_F2, X_F2, 3, False)
            rms(3)
            for k in range(KB):
                act.wait_ge(y_turned, k + 1)
                src = psum[:, 4 + k % 2, :]
                run(y_tok[:, 0:2, k * P:(k + 1) * P], src[:, 0:2 * P].rearrange("p (t n) -> p t n", n=P), ACT.Copy)
                run(y_tok[0:SAMP, 2, k * P:(k + 1) * P], src[0:SAMP, 2 * P:3 * P], ACT.Copy).then_inc(y_copied, 1)

        @block.vector
        def _(dve):
            v = nc.vector
            chained = [0]

            def chain(instruction):
                chained[0] += 1
                instruction.then_inc(dve_chain, 1)
                dve.wait_ge(dve_chain, chained[0])

            def split(u, turns=None, mod_unit=False):
                n = 1 if mod_unit else unit_floats(u)
                dve.wait_ge(hi_done, plus(u + 1, turns, RAW))
                v.tensor_tensor(lo_slot(u)[:, 0:n], raw_slot(u)[:, 0:n], hi_slot(u)[:, 0:n],
                                ALU.subtract).then_inc(lo_done, 1)

            def finished(u, turns=None):
                dve.wait_ge(unit_done, plus(u + 1, turns, RAW))

            def add_mod(group, place=None):
                place = group if place is None else place
                at = mod[:, bass.ds(place * 4, 4), :].rearrange("p (h c) n -> p h c n", c=2)
                src = psum[:, B_MODT, 0:2 * P].rearrange("p (c j h n) -> p j h c n", c=2, j=2, h=2)[:, :, :, :, 0:NC_]
                bias = prm[:, bass.ds(place * 4 + C_ADAB, 4)].rearrange("p (h c) -> p h c", c=2)
                bias = bias.unsqueeze(3).broadcast_to((P, 2, 2, NC_))
                dve.wait_ge(mod_turned, group + 1)
                v.tensor_tensor(at, src[:, 0], bias, ALU.add).then_inc(mod_half, 1)
                dve.wait_ge(mod_half, group + 1)
                v.tensor_tensor(at, at, src[:, 1], ALU.add).then_inc(mod_done, 1)

            for u in range(SPLIT):
                split(u, None, True)
            dve.wait_ge(c_turned, 1)
            src = psum[:, 5, 0:NC_ * KB].rearrange("p (k c) -> p k c", c=NC_)
            v.memset(c_t[:, :, NC_:32], 0.0)
            v.tensor_copy(c_t[:, :, 0:NC_], src).then_inc(c_ready, 1)
            def scale(n, vector, k0, blocks, groups):
                at = mod[:, KB * vector + k0:KB * vector + k0 + blocks, :]
                w = prm[:, C_NORM + KB * n + k0:C_NORM + KB * n + k0 + blocks].unsqueeze(2).broadcast_to((P, blocks, NC_))
                dve.wait_ge(mod_done, groups)
                v.scalar_tensor_tensor(out=at, in0=at, scalar=1.0, in1=w, op0=ALU.add, op1=ALU.mult).then_inc(scale_ready, 1)

            def normed(n, sc, k):
                dve.wait_ge(rstd_ready, n + 1)
                dve.wait_ge(scale_ready, k // Q + 1 if n == 0 else 4 + n)
                if k >= 3:
                    dve.wait_ge(h_ready, H_BASE[n] + k - 2)
                v.scalar_tensor_tensor(out=xn[:, k % 3, 0:SEQ], in0=x[:, k, 0:SEQ], scalar=mod[:, KB * sc + k, 0:1],
                                       in1=rstd[:, 0:SEQ], op0=ALU.mult, op1=ALU.mult).then_inc(xn_ready, 1)

            def lo_part(n, sh, k):
                if k % Q == 0:
                    dve.wait_ge(samp_hi_ready, n * 4 + k // Q + 1)
                    v.tensor_tensor(h_lo[:, k:k + Q, SEQ:T], h_samp[:, k:k + Q, :], h_hi[:, k:k + Q, SEQ:T],
                                    ALU.subtract).then_inc(samp_lo_ready, 1)
                    dve.wait_ge(samp_lo_ready, n * 4 + k // Q + 1)
                dve.wait_ge(h_hi_ready, H_BASE[n] + k + 1)
                v.scalar_tensor_tensor(out=h_lo[:, k, 0:SEQ], in0=xn[:, k % 3, 0:SEQ], scalar=mod[:, KB * sh + k, 0:1],
                                       in1=h_hi[:, k, 0:SEQ], op0=ALU.add, op1=ALU.subtract).then_inc(h_ready, 1)

            def modulate(n, sc, sh, first, end):
                for k in range(first, end + 2):
                    if k < end:
                        normed(n, sc, k)
                    if k - 2 >= first:
                        lo_part(n, sh, k - 2)

            def parameters():
                dve.wait_ge(prm_turned, 1)
                v.tensor_copy(prm[:, 0:2 * P], psum[:, B_NORM, 0:2 * P])
                v.tensor_copy(prm[:, 2 * P:2 * P + 16], psum[:, B_MODT, 0:16])
                v.tensor_copy(prm[:, C_SCONV:N_PRM], psum[:, B_NORM, 2 * P:4 * P]).then_inc(prm_ready, 1)
                dve.wait_ge(prm_ready, 1)

            def lru_constants():
                lam = prm[:, C_LAM:C_LAM + LH]
                chain(v.tensor_scalar(sp_s, lam, -1.0, None, ALU.mult))
                v.tensor_tensor(sp_e, lam, sp_s, ALU.max).then_inc(sp_ready, 1)
                dve.wait_ge(sp_exp, 1)
                chain(v.tensor_scalar(sp_q, sp_e, 2.0, None, ALU.add))
                chain(v.reciprocal(sp_q, sp_q))
                chain(v.tensor_tensor(sp_e, sp_e, sp_q, ALU.mult))
                chain(v.tensor_tensor(sp_s, sp_e, sp_e, ALU.mult))
                chain(v.tensor_scalar(sp_q, sp_s, 1.0 / 15, None, ALU.mult))
                for odd in (13, 11, 9, 7, 5, 3):
                    chain(v.scalar_tensor_tensor(out=sp_q, in0=sp_q, scalar=1.0 / odd, in1=sp_s, op0=ALU.add, op1=ALU.mult))
                chain(v.scalar_tensor_tensor(out=sp_q, in0=sp_q, scalar=1.0, in1=sp_e, op0=ALU.add, op1=ALU.mult))
                chain(v.tensor_scalar(sp_s, lam, -1.0, 0.0, ALU.mult, ALU.max))
                chain(v.scalar_tensor_tensor(out=sp_s, in0=sp_q, scalar=2.0, in1=sp_s, op0=ALU.mult, op1=ALU.add))
                v.tensor_scalar(m2sp, sp_s, -2.0, None, ALU.mult)
                v.tensor_scalar(m4sp, sp_s, -4.0, None, ALU.mult)
                v.tensor_scalar(half_ba, prm[:, C_BA:C_BA + LH], 0.5, None, ALU.mult)
                v.tensor_scalar(half_bx, prm[:, C_BX:C_BX + LH], 0.5, None, ALU.mult)
                v.tensor_copy(final_norm, prm[:, C_NORM + 3 * KB:C_NORM + 4 * KB])
            for u in range(U_F1):
                finished(u)
                if u % 8 == 7:
                    group = u // 8
                    if group == 0:
                        parameters()
                    add_mod(group, group // 2 + group % 2 * Q)
                    if group % 2:
                        scale(0, 1, group // 2 * Q, Q, group + 1)
                if u - 2 in MOD_AT:
                    lo_part(0, 0, MOD_AT.index(u - 2))
                if u in MOD_AT:
                    normed(0, 1, MOD_AT.index(u))
                split(u + SPLIT, None, u + SPLIT < U_F1 or u % 2 == 0)
                if u == 8:
                    lru_constants()
            modulate(0, 1, 0, 3 * Q, KB)

            def update(m, g, vector, before):
                gate = mod[:, bass.ds(m + KB * vector, 1), :].rearrange("p a c -> p (a c)")
                xm = x[:, bass.ds(m, 1), :].rearrange("p a n -> p (a n)")
                src = bank(g)
                v.scalar_tensor_tensor(out=xm[:, 0:SEQ], in0=src[:, 0:SEQ], scalar=gate[:, 0:1], in1=xm[:, 0:SEQ],
                                       op0=ALU.mult, op1=ALU.add)
                v.tensor_tensor(sample(prod[:, g % 2, :]), sample(src), gate[:, 1:NC_].unsqueeze(2).broadcast_to((P, NB, DS)),
                                ALU.mult).then_inc(dve_freed, 1)
                dve.wait_ge(dve_freed, before + 1)
                v.tensor_tensor(xm[:, SEQ:T], xm[:, SEQ:T], prod[:, g % 2, SEQ:T], ALU.add).then_inc(x_done, 1)

            def ffn(u0, g0, a0, vector, freed_before, with_mod):
                def hidden(step, g, gturns, block_of, count):
                    dve.wait_ge(silu_ready, count + 1)
                    v.scalar_tensor_tensor(out=prod[:, step % 2, :], in0=silu_g[:, step % 2, :], scalar=0.5,
                                           in1=bank(g + 1), op0=ALU.mult, op1=ALU.mult).then_inc(dve_freed, 2)
                    dve.wait_ge(dve_freed, plus(g + 2 - freed_before, gturns, ACC))
                    dst_hi = a_hi[:, bass.ds(block_of, 1), :].rearrange("p a n -> p (a n)")
                    dst_lo = a_lo[:, bass.ds(block_of, 1), :].rearrange("p a n -> p (a n)")
                    v.tensor_copy(dst_hi, prod[:, step % 2, :]).then_inc(a_hi_ready, 1)
                    dve.wait_ge(a_hi_ready, count + 1)
                    v.tensor_tensor(dst_lo, prod[:, step % 2, :], dst_hi, ALU.subtract).then_inc(a_ready, 1)

                def up_pair(u, turns, g, gturns, first_block, count, group, last_mod):
                    for n in range(8):
                        if group is not None:
                            finished(u, turns)
                            split(u + SPLIT, turns, not last_mod)
                            u += 1
                        finished(u, turns)
                        if group is None and n % 4 == 2:
                            finished(u + 1, turns)
                        if n % 4 == (2 if group is None else 3):
                            hidden(n // 4, g, gturns, first_block + n // 4, count + n // 4)
                            g += 2
                        if n == 7 and group is not None:
                            add_mod(group)
                        split(u + SPLIT, turns)
                        u += 1

                def down_eight(u, turns, g, gturns, m, group):
                    for n in range(8):
                        if group is not None:
                            finished(u, turns)
                            split(u + SPLIT, turns, True)
                            u += 1
                        finished(u, turns)
                        update(m + n, g, vector, plus(g - freed_before, gturns, ACC))
                        g += 1
                        if group is not None and n == 7:
                            add_mod(group)
                        split(u + SPLIT, turns)
                        u += 1

                def chunk(u, turns, g, gturns, count, group, mod_up, mod_down):
                    per = 2 if mod_up else 1
                    with dve.Fori(0, 4) as i:
                        up_pair(u, turns + i * per, g, gturns + i, i * 2, count + i * 2, group + i if mod_up else None,
                                not mod_down)
                    u, g = u + CB * 4 * per, g + 2 * CB
                    per = 2 if mod_down else 1
                    dve.wait_ge(mod_done, 4 * (vector + 1))
                    with dve.Fori(0, 2) as i:
                        down_eight(u, turns + i * per, g, gturns + i * 2, i * 8, group + 4 + i if mod_down else None)
                    return u + KB * per, g + KB

                if with_mod:
                    with dve.Fori(0, 4) as c:
                        chunk(u0, c * 12, g0, c * 8, c * CB + a0, c * 6 + 8, True, True)
                    scale(1, 4, 0, KB, 32)
                    scale(2, 7, 0, KB, 32)
                    u, g = chunk(u0 + 4 * 96, 0, g0 + 4 * CH_G, 0, a0 + 4 * CB, 32, True, False)
                else:
                    with dve.Fori(0, CHUNKS) as c:
                        chunk(u0, c * 6, g0, c * 8, c * CB + a0, 0, False, False)
                    u, g = u0 + CHUNKS * CH_U, g0 + CHUNKS * CH_G
                for s in range(TAIL):
                    for n in range(4):
                        finished(u)
                        if n == 3:
                            hidden(s, g, None, s, a0 + CHUNKS * CB + s)
                        split(u + SPLIT)
                        u += 1
                    g += 2
                for n in range(KB // 2):
                    finished(u)
                    for m in range(2):
                        update(2 * n + m, g, vector, g - freed_before)
                        g += 1
                    if u + SPLIT < U_END:
                        split(u + SPLIT)
                    u += 1

            ffn(U_F1, G_F1, 0, 2, 0, True)
            dve.wait_ge(sinks_in, 16)
            dve.wait_ge(tables_in, 16)
            for kv in range(NKV):
                chain(v.tensor_tensor(sink_pick, sinks[:, GRP * kv:GRP * (kv + 1)], group_of, ALU.mult))
                chain(v.reduce_sum(sink_s[:, kv:kv + 1], sink_pick, AX.X))

            modulate(1, 4, 3, 0, KB)

            def evacuate(n):
                kind, kv, h = MIX_KIND[n]
                src = bank(MIX_GROUP[n])
                if kind == "v":
                    v.tensor_copy(v_t[:, kv, :], src).then_inc(dve_freed, 1)
                if kind in "kq":
                    r = kv if kind == "k" else NKV + GRP * kv + h
                    dve.wait_ge(swapped_ready, r + 1)
                    v.tensor_tensor(rope_c, src, cos, ALU.mult)
                    v.tensor_tensor(rope_s, swapped, sin, ALU.mult).then_inc(dve_freed, 1)
                    dve.wait_ge(dve_freed, MIX_FREED[MIX_GROUP[n] - G_MIX][1])
                    if kind == "k":
                        v.tensor_tensor(k_t[:, kv, :], rope_c, rope_s, ALU.add).then_inc(rope_done, 1)
                    else:
                        v.tensor_tensor(q_p[:, h, :], rope_c[:, 0:SEQ], rope_s[:, 0:SEQ], ALU.add)
                        v.tensor_tensor(q_s[:, :, h, :], sample(rope_c), sample(rope_s), ALU.add).then_inc(rope_done, 1)

            conv_state = prm[:, C_SCONV:C_SCONV + NB * 3 * LH].rearrange("p (b j k) -> p b j k", j=3, k=LH)
            new_conv_s = st[:, 0:192].rearrange("p (b j k) -> p b j k", j=3, k=LH)
            new_conv_p = st[:, 256:280].rearrange("p (j k) -> p j k", k=LH)

            def convolve(head):
                xc = xc2[:, head % 2, :]
                if head > 1:
                    dve.wait_ge(gates_ready, head - 1)
                    dve.wait_ge(lru_done, head - 1)
                dve.wait_ge(xb_state, head + 2)
                dve.wait_ge(act_freed, 4 * head + 1)
                w = [prm[:, C_CW + j * LH + head:C_CW + j * LH + head + 1] for j in range(CONV)]
                b = prm[:, C_CB + head:C_CB + head + 1]
                v.tensor_copy(new_conv_s[:, :, :, head], xb_s[:, :, DS:DS + 3])
                v.tensor_copy(new_conv_p[:, :, head], xb_p[:, SEQ:SEQ + 3])
                v.tensor_scalar(xc[:, 0:SEQ], xb_p[:, 0:SEQ], w[0], b, ALU.mult, ALU.add)
                chain(v.tensor_scalar(sample(xc), xb_s[:, :, 0:DS], w[0], b, ALU.mult, ALU.add))
                for j in range(1, CONV):
                    v.scalar_tensor_tensor(out=xc[:, 0:SEQ], in0=xb_p[:, j:j + SEQ], scalar=w[j], in1=xc[:, 0:SEQ],
                                           op0=ALU.mult, op1=ALU.add)
                    last = v.scalar_tensor_tensor(out=sample(xc), in0=xb_s[:, :, j:j + DS], scalar=w[j], in1=sample(xc),
                                                  op0=ALU.mult, op1=ALU.add)
                    if j < CONV - 1:
                        chain(last)
                last.then_inc(xc_ready, 1)

            def recurrence(head):
                dve.wait_ge(gate_acts, head + 1)
                v.scalar_tensor_tensor(out=root[:, 0:SEQ], in0=a_p, scalar=1.0, in1=root[:, 0:SEQ], op0=ALU.add, op1=ALU.mult)
                chain(v.scalar_tensor_tensor(out=sample(root), in0=a_s[:, :, 1:1 + DS], scalar=1.0, in1=sample(root),
                                             op0=ALU.add, op1=ALU.mult))
                chain(v.scalar_tensor_tensor(out=root, in0=th_x, scalar=1.0, in1=root, op0=ALU.add, op1=ALU.mult))
                xc = xc2[:, head % 2, :]
                dve.wait_ge(xc_ready, head + 1)
                v.tensor_tensor(u_p, root[:, 0:SEQ], xc[:, 0:SEQ], ALU.mult)
                v.tensor_copy(u_s[:, :, 0], prm[:, C_SLRU:C_SLRU + NB * LH].rearrange("p (b k) -> p b k", k=LH)[:, :, head])
                chain(v.tensor_tensor(u_s[:, :, 1:1 + DS], sample(root), sample(xc), ALU.mult))
                if head:
                    dve.wait_ge(state_saved, head)
                v.tensor_tensor_scan(hs_p, a_p, u_p, 0.0, ALU.mult, ALU.add)
                chain(v.tensor_tensor_scan(hs_s.rearrange("p b s -> p (b s)"), a_s.rearrange("p b s -> p (b s)"),
                                           u_s.rearrange("p b s -> p (b s)"), 0.0, ALU.mult, ALU.add))
                dve.wait_ge(gelu_ready, head + 1)
                v.scalar_tensor_tensor(out=mix[:, head, 0:SEQ], in0=gel[:, 0:SEQ], scalar=0.5, in1=hs_p,
                                       op0=ALU.mult, op1=ALU.mult)
                v.scalar_tensor_tensor(out=sample(mix[:, head, :]), in0=sample(gel), scalar=0.5, in1=hs_s[:, :, 1:1 + DS],
                                       op0=ALU.mult, op1=ALU.mult).then_inc(lru_done, 1)

            def copy_tokens(kv):
                dve.wait_ge(tok_turned, kv + 1)
                src = psum[:, B_TOK, :]
                v.tensor_copy(tok[:, 0, kv, :], src[:, 0:P])
                v.tensor_copy(tok[:, 1, kv, :], src[:, P:2 * P])
                v.tensor_copy(tok[:, 3, kv, :], src[:, 2 * P:3 * P])
                v.tensor_copy(tok[0:SAMP, 2, kv, :], src[0:SAMP, 3 * P:4 * P])
                v.tensor_copy(tok[0:SAMP, 4, kv, :], psum[0:SAMP, B_O, 0:P]).then_inc(tok_ready, 1)

            def softmax_head(kv, t):
                job = 6 * kv + t
                dve.wait_ge(scored, job + 1)
                n, mask = (3 * P, mask_p) if t < GRP else (P + SAMP, mask_s[t - GRP])
                v.scalar_tensor_tensor(out=score[:, 0:n], in0=psum[:, B_SCORE, 0:n], scalar=SCALE, in1=mask,
                                       op0=ALU.mult, op1=ALU.add).then_inc(masked, 1)
                dve.wait_ge(masked, job + 1)
                if t < GRP:
                    v.reduce_max(top[:, 0:1], score[:, 0:P], AX.X)
                    chain(v.reduce_max(top[:, 1:2], score[:, P:3 * P], AX.X))
                    head = GRP * kv + t
                    v.tensor_scalar(neg_top, top, sinks[:, head:head + 1], -1.0, ALU.max, ALU.mult).then_inc(maxed, 1)
                else:
                    chain(v.reduce_max(top[:, 0:1], score[:, 0:n], AX.X))
                    v.tensor_scalar(neg_top[:, 0:1], top[:, 0:1], sink_s[:, kv:kv + 1], -1.0, ALU.max,
                                    ALU.mult).then_inc(maxed, 1)

            def softmax_tail(kv, t):
                job = 6 * kv + t
                dve.wait_ge(exp_done, job + 1)
                m = 2 if t < GRP else 1
                chain(v.tensor_tensor(den[:, 0:m], den[:, 0:m], sink_e[:, 0:m], ALU.add))
                chain(v.reciprocal(den[:, 0:m], den[:, 0:m]))
                if t < GRP:
                    v.tensor_scalar(score[:, 0:P], score[:, 0:P], den[:, 0:1], None, ALU.mult)
                    v.tensor_scalar(score[:, P:3 * P], score[:, P:3 * P], den[:, 1:2], None, ALU.mult).then_inc(probs_ready, 1)
                else:
                    v.tensor_scalar(score[:, 0:P + SAMP], score[:, 0:P + SAMP], den[:, 0:1], None,
                                    ALU.mult).then_inc(probs_ready, 1)

            def behind(n):
                kind, kv, h = MIX_KIND[n]
                if kind == "q" and h < 2 and kv == 0:
                    copy_tokens(h)
                t = 2 * h + (kind == "y")
                attends = kind in ("x", "y") and t < 6
                if attends:
                    softmax_head(kv, t)
                if kind == "x":
                    convolve(GRP * kv + h)
                if attends:
                    softmax_tail(kv, t)

            def operand(first, end):
                for k in range(first, end):
                    dve.wait_ge(h_hi_ready, 2 * KB + (k + LH) % KB + 1)
                    v.tensor_tensor(h_lo[:, k, :], mix[:, k, :], h_hi[:, k, :], ALU.subtract).then_inc(h_ready, 1)

            for n in range(MIX_BLOCKS):
                finished(U_MIX + 2 * n)
                if n == 1:
                    evacuate(0)
                split(U_MIX + 2 * n + SPLIT)
                finished(U_MIX + 2 * n + 1)
                if n:
                    evacuate(n)
                behind(n)
                if n == MIX_BLOCKS - 1:
                    operand(LH, KB)
                split(U_MIX + 2 * n + 1 + SPLIT)
                if MIX_KIND[n][0] == "y" and n < MIX_BLOCKS - 1:
                    recurrence(GRP * MIX_KIND[n][1] + MIX_KIND[n][2])

            operand(0, LH - 1)
            recurrence(LH - 1)
            operand(LH - 1, LH)

            with dve.Fori(0, 4) as i:
                for n in range(8):
                    finished(U_OUT + n, i)
                    if n >= 4:
                        update(i * 4 + n - 4, G_OUT + n - 4, 5, plus(G_OUT + n - 4 - ACT_FREED, i, ACC))
                    split(U_OUT + n + SPLIT, i)
            modulate(2, 7, 6, 0, KB)
            ffn(U_F2, G_F2, FB, 8, ACT_FREED, False)

            dve.wait_ge(rstd_ready, 4)
            for k in range(KB):
                if k >= 3:
                    dve.wait_ge(y_turned, k - 2)
                v.scalar_tensor_tensor(out=xn[:, k % 3, :], in0=x[:, k, :], scalar=final_norm[:, k:k + 1], in1=rstd,
                                       op0=ALU.mult, op1=ALU.mult).then_inc(xn_y, 1)

        @block.gpsimd
        def _(pool):
            g = nc.gpsimd
            chained = [0]

            def chain(instruction):
                chained[0] += 1
                instruction.then_inc(pool_chain, 1)
                pool.wait_ge(pool_chain, chained[0])

            g.memset(ones, 1.0).then_inc(set_up, 1)
            g.memset(eps, EPS).then_inc(set_up, 1)
            g.memset(a_s[:, :, 0:1], 0.0)
            row = 0
            for name in ('norm_ffn1', 'norm_mix', 'norm_ffn2'):
                pool.dma_start(prm_tok[row:row + KB, 0, :], io[name].rearrange("a (k n) -> (a k) n", n=P)).then_inc(prm_in, 16)
                row += KB
            pool.dma_start(prm_tok[row:row + KB, 0, :], io['norm_final'].rearrange("(k n) -> k n", n=P)).then_inc(prm_in, 16)
            row += KB
            pool.dma_start(prm_tok[row:row + 32, 0, :], io['conv_w'][0].rearrange("j (k n) -> (j k) n", n=P)).then_inc(prm_in, 16)
            row += 32
            pool.dma_start(prm_tok[row:row + 8, 0, :], io['conv_b'].rearrange("a (k n) -> (a k) n", n=P)).then_inc(prm_in, 16)
            pool.dma_start(prm_tok[row + 8:row + 16, 0, :], io['lru_b_a'][0]).then_inc(prm_in, 16)
            pool.dma_start(prm_tok[row + 16:row + 24, 0, :], io['lru_b_x'][0]).then_inc(prm_in, 16)
            pool.dma_start(prm_tok[row + 24:row + 32, 0, :], io['lru_lambda'].rearrange("a (k n) -> (a k) n", n=P)).then_inc(prm_in, 16)
            ada_b = io['ada_b'].rearrange("a (k n) -> (a k) n", n=P)
            pool.dma_start(prm_tok[:, 1, :], ada_b[0:P]).then_inc(prm_in, 16)
            pool.dma_start(prm_tok[0:16, 4, :], ada_b[P:P + 16]).then_inc(prm_in, 16)
            conv = io['state_conv'][0].rearrange("b j (k n) -> (b j k) n", n=P)
            pool.dma_start(prm_tok[:, 2, :], conv[0:P]).then_inc(prm_in, 16)
            pool.dma_start(prm_tok[0:64, 3, :], conv[P:192]).then_inc(prm_in, 16)
            pool.dma_start(prm_tok[64:128, 3, :], io['state_lru'][0].rearrange("b (k n) -> (b k) n", n=P)).then_inc(prm_in, 16)

            def load_cached_keys(kv):
                src = io['cache_k_win'][0, :, :, kv, :].rearrange("b s d -> s b d")
                pool.dma_start(ck_tok, src).then_inc(ck_in, 16)

            def load_cached_values(kv):
                src = io['cache_v_win'][0, :, :, kv, :].rearrange("b s d -> s b d")
                pool.dma_start(cv_tok, src).then_inc(cv_in, 16)

            def load_gates(kv):
                heads = slice(GRP * kv, GRP * (kv + 1))
                pool.dma_start(w_a, io['lru_w_a'][0, heads].rearrange("h i j -> i h j")).then_inc(gates_in, 16)
                pool.dma_start(w_x, io['lru_w_x'][0, heads].rearrange("h i j -> i h j")).then_inc(gates_in, 16)

            def add_squares(n):
                for m in range(KB):
                    pool.wait_ge(squared, n * KB + m + 1)
                    if m == 0:
                        if n:
                            pool.wait_ge(ms_ready, n)
                        g.tensor_copy(sum_sq, sq[:, 0, :]).then_inc(summed, 1)
                    else:
                        pool.wait_ge(summed, n * KB + m)
                        g.tensor_tensor(sum_sq, sum_sq, sq[:, m % 2, :], ALU.add).then_inc(summed, 1)

            def samples(n, sc, sh):
                vec = (lambda at, k: mod[:, KB * at + k:KB * at + k + Q, 1:NC_].unsqueeze(3).broadcast_to((P, Q, NB, DS)))
                for q in range(4):
                    pool.wait_ge(scale_ready, q + 1 if n == 0 else 4 + n)
                    k = q * Q
                    out = h_samp[:, k:k + Q, :].rearrange("p k (b s) -> p k b s", s=DS)
                    chain(g.tensor_tensor(out, x[:, k:k + Q, SEQ:T].rearrange("p k (b s) -> p k b s", s=DS), vec(sc, k),
                                          ALU.mult))
                    if q == 0:
                        pool.wait_ge(rstd_ready, n + 1)
                    chain(g.tensor_tensor(h_samp[:, k:k + Q, :], h_samp[:, k:k + Q, :],
                                          rstd[:, SEQ:T].unsqueeze(1).broadcast_to((P, Q, SAMP)), ALU.mult))
                    g.tensor_tensor(out, out, vec(sh, k), ALU.add).then_inc(samp_ready, 1)

            add_squares(0)
            samples(0, 1, 0)
            pool.wait_ge(unit_done, U_F1)
            pool.dma_start(sinks, io['attn_sinks'].broadcast_to((P, NH))).then_inc(sinks_in, 16)
            pool.dma_start(tables, io['tables']).then_inc(tables_in, 16)
            load_cached_keys(0)
            load_cached_values(0)
            load_gates(0)
            for new, old in (('k_sample', 'cache_k_win'), ('v_sample', 'cache_v_win')):
                pool.dma_start(io[new][0, :, 0:WIN - DS].rearrange("b s h d -> b (s h d)"),
                               io[old][0, :, DS:WIN].rearrange("b s h d -> b (s h d)")).then_inc(cache_stored, 16)

            add_squares(1)
            samples(1, 4, 3)

            conv_state = prm[:, C_SCONV:C_SCONV + NB * 3 * LH].rearrange("p (b j k) -> p b j k", j=3, k=LH)
            new_lru_s = st[:, 192:256].rearrange("p (b k) -> p b k", k=LH)
            new_lru_p = st[:, 280:288]

            def old_state(head):
                if head == 0:
                    pool.wait_ge(tok_turned, NKV)
                    g.memset(xb_p[:, 0:3], 0.0).then_inc(xb_state, 1)
                else:
                    pool.wait_ge(xc_ready, head)
                g.tensor_copy(xb_s[:, :, 0:3], conv_state[:, :, :, head]).then_inc(xb_state, 1)

            def save_state(head):
                pool.wait_ge(lru_done, head + 1)
                g.tensor_copy(new_lru_s[:, :, head], hs_s[:, :, DS])
                g.tensor_copy(new_lru_p[:, head:head + 1], hs_p[:, SEQ - 1:SEQ]).then_inc(state_saved, 1)

            for head in range(LH):
                old_state(head)
                if head == 1:
                    pool.wait_ge(ck_turned, 2)
                    load_cached_keys(1)
                pool.wait_ge(act_freed, 4 * head + 2)
                chain(g.tensor_scalar(gel, gel, 0.044715, 1.0, ALU.mult, ALU.add))
                g.tensor_tensor(gel, gel, yf, ALU.mult).then_inc(gel_z, 1)
                pool.wait_ge(gel_t, head + 1)
                chain(g.tensor_scalar(gel, gel, 1.0, None, ALU.add))
                g.tensor_tensor(gel, gel, yf, ALU.mult).then_inc(gelu_ready, 1)
                if head:
                    save_state(head - 1)
                if head == GRP - 1:
                    pool.wait_ge(gates_ready, GRP)
                    load_gates(1)
                    pool.wait_ge(o_ready, 6)
                    load_cached_values(1)
            save_state(LH - 1)
            pool.wait_ge(tok_stored, TOK_DMAS * 16)
            add_squares(2)
            samples(2, 7, 6)

            pool.wait_ge(st_copied, 1)
            conv_rows = io['conv_sample'][0].rearrange("b j (k n) -> (b j k) n", n=P)
            pool.dma_start(conv_rows[0:P], prm[:, 0:P]).then_inc(state_stored, 16)
            pool.dma_start(conv_rows[P:192], prm[0:64, P:2 * P]).then_inc(state_stored, 16)
            pool.dma_start(io['lru_sample'][0].rearrange("b (k n) -> (b k) n", n=P), prm[64:P, P:2 * P]).then_inc(state_stored, 16)
            pool.dma_start(io['conv_prompt'][0, 0].rearrange("j (k n) -> (j k) n", n=P), prm[0:24, 2 * P:3 * P]).then_inc(state_stored, 16)
            pool.dma_start(io['lru_prompt'][0].rearrange("a (k n) -> (a k) n", n=P), prm[24:32, 2 * P:3 * P]).then_inc(state_stored, 16)
            add_squares(3)


def shape_constants(np):
    i, j = np.arange(P)[:, None], np.arange(2 * P)[None, :]
    never = np.float32(-1e30)
    t = np.zeros((P, 6 * P + 4 + 2 * T), np.float32)
    t[:, 0:P] = np.where(j[:, :P] <= i, 0, never)
    t[:, P:3 * P] = np.where((j <= P + i) & (j >= i), 0, never)
    step, seq = i % DS, i // (GRP * DS)
    new = np.arange(SAMP)[None, :]
    for half in range(2):
        m = t[:, 3 * P + (P + SAMP) * half:3 * P + (P + SAMP) * (half + 1)]
        m[:, 0:P] = np.where(j[:, :P] >= step, 0, never)
        m[:, P:] = np.where((new // DS == 4 * half + seq) & (new % DS <= step), 0, never)
    t[:, 6 * P:6 * P + 4] = (i // DS % GRP == np.arange(GRP)[None, :])
    pos = np.concatenate([np.arange(SEQ), np.tile(PAST + np.arange(DS), NB)]).astype(np.float32)
    inv = (np.float32(10000.0) ** (-np.arange(64, dtype=np.float32) / np.float32(64))).astype(np.float32)
    ang = inv[:, None] * pos[None, :]
    c, s = np.cos(ang), np.sin(ang)
    t[:, 6 * P + 4:6 * P + 4 + T] = np.concatenate([c, c])
    t[:, 6 * P + 4 + T:] = np.concatenate([-s, s])
    return {'identity': np.eye(P, dtype=np.float32), 'tables': t}


def kernel(**inputs):
    import numpy as np
    import concourse.bacc as bacc
    from concourse.bass_utils import run_bass_kernel_spmd

    nc = bacc.Bacc("TRN2", target_bir_lowering=False, num_devices=1)
    data = {**inputs, **shape_constants(np)}
    arrays, io = {}, {}
    for name in INS:
        a = np.ascontiguousarray(data[name])
        arrays[f"in_{name}"] = a
        io[name] = nc.dram_tensor(f"in_{name}", a.shape, mybir.dt.from_np(a.dtype), kind="ExternalInput").ap()
    for name, shape in OUTS:
        io[name] = nc.dram_tensor(f"out_{name}", shape, F32, kind="ExternalOutput").ap()
    build(nc, io)
    r = run_bass_kernel_spmd(nc, [arrays], core_ids=[0])
    return tuple(r.results[0][f"out_{name}"] for name, _ in OUTS)
```
